# Optimizing a Trainium2 kernel written in Bass

```python
import jax
import jax.numpy as jnp
from jax import lax
import numpy as np

D_MODEL = 1024
BATCH = 1
SEQ = 512
DEPTH = 2

GRID_W = 64
CTX_LEN = 256
N_MIXERS = 4
GROUP_WIDTH = D_MODEL // N_MIXERS
D_MIX = N_MIXERS * GROUP_WIDTH
HEAD_DIM = 64
BLOCK = 128
ROPE_THETA = 10000.0
EPS = 1e-6
NEG_INF = -1e30
N_MOD = 6
A_HEADS = GROUP_WIDTH // HEAD_DIM
A_KV_HEADS = 2
WINDOW = 128
POOL_SIZES = (2, 4, 8, 16)
POOL_GROUP = GROUP_WIDTH // len(POOL_SIZES)
C_NOPE = 64
C_ROPE = 32
C_V = 64
C_HEADS = GROUP_WIDTH // C_V
C_Q_RANK = D_MODEL // 4
C_KV_RANK = D_MODEL // 8
D_HEADS = GROUP_WIDTH // HEAD_DIM
D_KV_HEADS = 2
D_FF = -(-(8 * D_MODEL) // (3 * 256)) * 256

IN_WIDTHS = (A_HEADS * HEAD_DIM, A_KV_HEADS * HEAD_DIM, A_KV_HEADS * HEAD_DIM,
             GROUP_WIDTH,
             C_Q_RANK, C_KV_RANK, C_ROPE,
             D_HEADS * HEAD_DIM, D_KV_HEADS * HEAD_DIM, D_KV_HEADS * HEAD_DIM)
IN_SPLITS = tuple(int(v) for v in np.cumsum(IN_WIDTHS)[:-1])
IN_WIDTH = int(sum(IN_WIDTHS))

kernel_name = 'hybrid_parallel_group_flow_block'

def rms_norm(x, g):
    xf = x.astype(jnp.float32)
    y = xf * lax.rsqrt(jnp.mean(xf * xf, axis=-1, keepdims=True) + EPS)
    return (y * g.astype(jnp.float32)).astype(x.dtype)

def axial_rope(row, col, rot_dim):
    n_axis = rot_dim // 4
    freqs = ROPE_THETA ** (-jnp.arange(n_axis, dtype=jnp.float32) / n_axis)
    ang = jnp.concatenate([row[:, None] * freqs, col[:, None] * freqs], axis=-1)
    return jnp.cos(ang), jnp.sin(ang)

def apply_rope(x, rope):
    cos, sin = rope
    cos = cos[None, :, None, :].astype(x.dtype)
    sin = sin[None, :, None, :].astype(x.dtype)
    half = x.shape[-1] // 2
    x1, x2 = x[..., :half], x[..., half:]
    return jnp.concatenate([x1 * cos - x2 * sin, x2 * cos + x1 * sin], axis=-1)

def softmax_with_sink(s, sink):
    m = jnp.maximum(jnp.max(s, axis=-1, keepdims=True), sink)
    p = jnp.exp(s - m)
    return p / (jnp.sum(p, axis=-1, keepdims=True) + jnp.exp(sink - m))

def modulation(cond, w, b):
    m = jax.nn.silu(cond) @ w + b
    return jnp.split(m[:, None, :], N_MOD, axis=-1)

def modulate(h, shift, scale):
    return h * (1 + scale) + shift

def full_attention(q, k, v, scale, sink=None):
    b, tq, h, d = q.shape
    hk = k.shape[2]
    qg = q.reshape(b, tq, hk, h // hk, d)
    s = jnp.einsum('bqhgd,bkhd->bhgqk', qg, k, preferred_element_type=jnp.float32) * scale
    if sink is None:
        w = jax.nn.softmax(s, axis=-1)
    else:
        w = softmax_with_sink(s, sink.astype(jnp.float32).reshape(1, hk, h // hk, 1, 1))
    o = jnp.einsum('bhgqk,bkhd->bqhgd', w.astype(v.dtype), v)
    return o.reshape(b, tq, h * v.shape[-1])

def dense_attention(q, k, v, k_ctx, v_ctx, scale):
    b, n, h, d = q.shape
    hk = k.shape[2]
    g = h // hk
    keys = jnp.concatenate([k_ctx, k], axis=1)
    vals = jnp.concatenate([v_ctx, v], axis=1)
    qb = jnp.moveaxis(q.reshape(b, n // BLOCK, BLOCK, hk, g, d), 1, 0)

    def one_block(qi):
        s = jnp.einsum('bqhgd,bkhd->bhgqk', qi, keys, preferred_element_type=jnp.float32) * scale
        w = jax.nn.softmax(s, axis=-1)
        return jnp.einsum('bhgqk,bkhd->bqhgd', w.astype(vals.dtype), vals)

    o = lax.map(one_block, qb)
    return jnp.moveaxis(o, 0, 1).reshape(b, n, h * vals.shape[-1])

def window_attention(q, k, v, k_ctx, v_ctx, sink, scale):
    b, n, h, d = q.shape
    hk = k.shape[2]
    g = h // hk
    nb = n // BLOCK

    def band(t):
        tb = t.reshape(b, nb, BLOCK, hk, t.shape[-1])
        tp = jnp.pad(tb, ((0, 0), (1, 1), (0, 0), (0, 0), (0, 0)))
        return jnp.concatenate([tp[:, :-2], tp[:, 1:-1], tp[:, 2:]], axis=2)

    kb, vb = band(k), band(v)
    qb = q.reshape(b, nb, BLOCK, hk, g, d)
    blk = jnp.arange(nb)[:, None]
    q_pos = blk * BLOCK + jnp.arange(BLOCK)[None, :]
    k_pos = (blk - 1) * BLOCK + jnp.arange(3 * BLOCK)[None, :]
    valid = ((jnp.abs(q_pos[:, :, None] - k_pos[:, None, :]) <= WINDOW)
             & (k_pos[:, None, :] >= 0) & (k_pos[:, None, :] < n))
    s_loc = jnp.einsum('bnqhgd,bnkhd->bnhgqk', qb, kb, preferred_element_type=jnp.float32) * scale
    s_loc = jnp.where(valid[None, :, None, None], s_loc, NEG_INF)
    s_ctx = jnp.einsum('bnqhgd,bkhd->bnhgqk', qb, k_ctx, preferred_element_type=jnp.float32) * scale
    n_ctx = k_ctx.shape[1]
    w = softmax_with_sink(jnp.concatenate([s_ctx, s_loc], axis=-1),
                          sink.astype(jnp.float32).reshape(1, 1, hk, g, 1, 1)).astype(v.dtype)
    o = (jnp.einsum('bnhgqk,bkhd->bnqhgd', w[..., :n_ctx], v_ctx)
         + jnp.einsum('bnhgqk,bnkhd->bnqhgd', w[..., n_ctx:], vb))
    return o.reshape(b, n, h * v.shape[-1])

def multiscale_pool(u, w_pool, scale):
    b, t, _ = u.shape
    uf = u.astype(jnp.float32).reshape(b, t, len(POOL_SIZES), POOL_GROUP)
    csum = jnp.pad(jnp.cumsum(uf, axis=1), ((0, 0), (1, 0), (0, 0), (0, 0)))
    pos = jnp.arange(t)
    outs = []
    for gi, size in enumerate(POOL_SIZES):
        lo = jnp.clip(pos - size // 2, 0, t)
        hi = jnp.clip(pos - size // 2 + size, 0, t)
        mean = (csum[:, hi, gi] - csum[:, lo, gi]) / (hi - lo).astype(jnp.float32)[None, :, None]
        outs.append(mean - uf[:, :, gi])
    y = jnp.stack(outs, axis=2).astype(u.dtype)
    y = jnp.einsum('btgc,gce->btge', y, w_pool).reshape(b, t, GROUP_WIDTH)
    return y * scale

def mixer_inputs(h, w_in, c_gq, c_wuq, c_gkv, c_wukv, d_gq, d_gk, rope_hd, rope_c):
    b, t, _ = h.shape
    z = h @ w_in
    qa, ka, va, ub, cq, ckv, kr, qd, kd, vd = jnp.split(z, IN_SPLITS, axis=-1)
    qa = qa.reshape(b, t, A_HEADS, HEAD_DIM)
    ka = ka.reshape(b, t, A_KV_HEADS, HEAD_DIM)
    va = va.reshape(b, t, A_KV_HEADS, HEAD_DIM)
    qc = (rms_norm(cq, c_gq) @ c_wuq).reshape(b, t, C_HEADS, C_NOPE + C_ROPE)
    q_nope, q_rope = qc[..., :C_NOPE], qc[..., C_NOPE:]
    kvc = (rms_norm(ckv, c_gkv) @ c_wukv).reshape(b, t, C_HEADS, C_NOPE + C_V)
    k_nope, vc = kvc[..., :C_NOPE], kvc[..., C_NOPE:]
    k_rope = kr.reshape(b, t, 1, C_ROPE)
    qd = rms_norm(qd.reshape(b, t, D_HEADS, HEAD_DIM), d_gq)
    kd = rms_norm(kd.reshape(b, t, D_KV_HEADS, HEAD_DIM), d_gk)
    vd = vd.reshape(b, t, D_KV_HEADS, HEAD_DIM)
    if rope_hd is not None:
        qa, ka = apply_rope(qa, rope_hd), apply_rope(ka, rope_hd)
        qd, kd = apply_rope(qd, rope_hd), apply_rope(kd, rope_hd)
        q_rope, k_rope = apply_rope(q_rope, rope_c), apply_rope(k_rope, rope_c)
    qc = jnp.concatenate([q_nope, q_rope], axis=-1)
    kc = jnp.concatenate([k_nope, jnp.broadcast_to(k_rope, (b, t, C_HEADS, C_ROPE))], axis=-1)
    return qa, ka, va, ub, qc, kc, vc, qd, kd, vd

def swiglu(h, w_gu, w_down):
    gate, up = jnp.split(h @ w_gu, 2, axis=-1)
    return (jax.nn.silu(gate) * up) @ w_down

def setup_inputs(seed: int = 0) -> dict:
    key = jax.random.key(seed)
    ks = jax.random.split(key, 23)
    f32 = jnp.float32
    L, D = DEPTH, D_MODEL

    def nrm(k, shape, scale):
        return jax.random.normal(k, shape, f32) * scale

    def gain(k, shape):
        return 1.0 + 0.02 * jax.random.normal(k, shape, f32)

    return {
        'x': nrm(ks[0], (BATCH, SEQ, D), 1.0),
        'c': nrm(ks[1], (BATCH, D), 1.0),
        'ctx': nrm(ks[2], (BATCH, CTX_LEN, D), 1.0),
        'c_ctx': nrm(ks[3], (D,), 1.0),
        'w_ada': nrm(ks[4], (L, D, N_MOD * D), 0.5 * D ** -0.5),
        'b_ada': nrm(ks[5], (L, N_MOD * D), 0.02),
        'g_pre1': gain(ks[6], (L, D)),
        'g_post1': gain(ks[7], (L, D)),
        'w_in': nrm(ks[8], (L, D, IN_WIDTH), D ** -0.5),
        'a_sink': nrm(ks[9], (L, A_HEADS), 1.0),
        'pool_w': nrm(ks[10], (L, len(POOL_SIZES), POOL_GROUP, POOL_GROUP), POOL_GROUP ** -0.5),
        'pool_scale': gain(ks[11], (L, GROUP_WIDTH)),
        'c_gq': gain(ks[12], (L, C_Q_RANK)),
        'c_wuq': nrm(ks[13], (L, C_Q_RANK, C_HEADS * (C_NOPE + C_ROPE)), C_Q_RANK ** -0.5),
        'c_gkv': gain(ks[14], (L, C_KV_RANK)),
        'c_wukv': nrm(ks[15], (L, C_KV_RANK, C_HEADS * (C_NOPE + C_V)), C_KV_RANK ** -0.5),
        'd_gq': gain(ks[16], (L, HEAD_DIM)),
        'd_gk': gain(ks[17], (L, HEAD_DIM)),
        'w_out': nrm(ks[18], (L, D_MIX, D), D_MIX ** -0.5),
        'g_pre2': gain(ks[19], (L, D)),
        'g_post2': gain(ks[20], (L, D)),
        'w_gu': nrm(ks[21], (L, D, 2 * D_FF), D ** -0.5),
        'w_down': nrm(ks[22], (L, D_FF, D), D_FF ** -0.5),
    }

def reference(x, c, ctx, c_ctx, w_ada, b_ada, g_pre1, g_post1, w_in, a_sink, pool_w, pool_scale,
              c_gq, c_wuq, c_gkv, c_wukv, d_gq, d_gk, w_out, g_pre2, g_post2, w_gu, w_down):
    n = x.shape[1]
    rows = n // GRID_W
    row = jnp.repeat(jnp.arange(rows, dtype=jnp.float32), GRID_W)
    col = jnp.tile(jnp.arange(GRID_W, dtype=jnp.float32), rows)
    rope_hd = axial_rope(row, col, HEAD_DIM)
    rope_c = axial_rope(row, col, C_ROPE)
    scale_hd = HEAD_DIM ** -0.5
    scale_c = (C_NOPE + C_ROPE) ** -0.5

    for l in range(DEPTH):
        last = l == DEPTH - 1
        mx = modulation(c, w_ada[l], b_ada[l])
        mc = modulation(c_ctx[None], w_ada[l], b_ada[l])
        proj = (w_in[l], c_gq[l], c_wuq[l], c_gkv[l], c_wukv[l], d_gq[l], d_gk[l])

        hx = modulate(rms_norm(x, g_pre1[l]), mx[0], mx[1])
        hc = modulate(rms_norm(ctx, g_pre1[l]), mc[0], mc[1])
        qa, ka, va, ub, qc, kc, vc, qd, kd, vd = mixer_inputs(hx, *proj, rope_hd, rope_c)
        qa_c, ka_c, va_c, ub_c, qc_c, kc_c, vc_c, qd_c, kd_c, vd_c = mixer_inputs(hc, *proj, None, None)

        ya = window_attention(qa, ka, va, ka_c, va_c, a_sink[l], scale_hd)
        yb = multiscale_pool(ub, pool_w[l], pool_scale[l])
        yc = dense_attention(qc, kc, vc, kc_c, vc_c, scale_c)
        yd = dense_attention(qd, kd, vd, kd_c, vd_c, scale_hd)
        y = jnp.concatenate([ya, yb, yc, yd], axis=-1) @ w_out[l]
        x = x + mx[2] * rms_norm(y, g_post1[l])

        if not last:
            ya_c = full_attention(qa_c, ka_c, va_c, scale_hd, a_sink[l])
            yb_c = multiscale_pool(ub_c, pool_w[l], pool_scale[l])
            yc_c = full_attention(qc_c, kc_c, vc_c, scale_c)
            yd_c = full_attention(qd_c, kd_c, vd_c, scale_hd)
            y_c = jnp.concatenate([ya_c, yb_c, yc_c, yd_c], axis=-1) @ w_out[l]
            ctx = ctx + mc[2] * rms_norm(y_c, g_post1[l])

        hx = modulate(rms_norm(x, g_pre2[l]), mx[3], mx[4])
        x = x + mx[5] * rms_norm(swiglu(hx, w_gu[l], w_down[l]), g_post2[l])
        if not last:
            hc = modulate(rms_norm(ctx, g_pre2[l]), mc[3], mc[4])
            ctx = ctx + mc[5] * rms_norm(swiglu(hc, w_gu[l], w_down[l]), g_post2[l])

    return x


_drawn_inputs = setup_inputs


def setup_inputs(seed=0):
    import zlib

    import numpy as np

    out = dict(_drawn_inputs(seed))
    spreads = {}
    factors = {'g_pre1': 7.058,
     'g_post1': 6.791,
     'a_sink': 8.0,
     'pool_scale': 7.3,
     'c_gq': 8.0,
     'c_gkv': 8.0,
     'd_gq': 8.0,
     'd_gk': 8.0,
     'g_pre2': 5.314,
     'g_post2': 7.2}
    for name, (base, spread) in spreads.items():
        noise = np.random.default_rng([zlib.crc32(name.encode()), seed]).standard_normal(out[name].shape)
        drawn = base * np.exp(spread * noise) if base else spread * noise
        out[name] = jnp.asarray(drawn.astype(out[name].dtype))
    for name, factor in factors.items():
        out[name] = (out[name] * factor).astype(out[name].dtype)
    return out
```

```python
from contextlib import ExitStack

import concourse.bass as bass
from concourse import mybir

F32 = mybir.dt.float32
F32R = mybir.dt.float32r
BF16 = mybir.dt.bfloat16
ALU = mybir.AluOpType
ACT = mybir.ActivationFunctionType
AX = mybir.AxisListType

LAYERS = 2
P = 128
D = 1024
DC = D // P
CTX, LAT = 256, 512
TOK = CTX + LAT
NB = TOK // P
CB = CTX // P
FF = 2816
FG = (8, 8, 6)
N_IN, N_OUT = 14, DC
TILES = N_IN + N_OUT + sum(2 * j + DC for j in FG)
(VA, VD, CQ0, CQ1, CKV, KR, QD0, QD1, KD, QA0, QA1, KA, UB0, UB1) = range(N_IN)
EPS = 1e-6
PAD = 8
PW = PAD + CTX + 2 * PAD + LAT + PAD
ADA = 48
ADA_FIRST = 2 * DC
ADA_MID = 3 * DC
ADA_G = 4
MID_SLOTS = 6
NG = 4 * DC
PB_ADA = NG
PPS = PB_ADA + ADA
PGQ, PGKV, PDGQ, PDGK, PSINK = PPS + 2, PPS + 4, PPS + 5, PPS + 6, PPS + 7
NPAR = PSINK + 4
KID, KMEAN = 0, P
KINV = KMEAN + 5
KEDGE = KINV + 2
NCONST = KEDGE + 2 * 4 * PAD
RHD, RC = 0, 2

HEADS = ([("D", 8 + h, 18 + h // 2, 2 + h // 2, 64, 12 + h) for h in range(4)]
         + [("C", 4 + h, 14 + h, 4 + h, 96, 8 + h) for h in range(4)]
         + [("A", h, 12 + h // 2, h // 2, 64, h) for h in range(4)])
NH = len(HEADS)
SCALE = {"A": 64 ** -0.5, "C": 96 ** -0.5, "D": 64 ** -0.5}
KEYS = (0, 2, 3, 4, 5, 1)

AUX = ([("sum", "pre1"), ("bc", "pre1"), ("sum", "cq"), ("bc", "cq"), ("sum", "ckv"), ("bc", "ckv"),
        ("sum", "qd0")] + [("lq", h) for h in range(4)] + [("bc", "qd0"), ("sum", "qd1")]
       + [("lk", h) for h in range(4)] + [("lv", 0), ("lv", 1), ("bc", "qd1"), ("sum", "kd"), ("bc", "kd")])
AUX2 = [("sum", "post1"), ("bc", "post1"), ("sum", "pre2"), ("bc", "pre2")]
AUX3 = [("sum", "post2"), ("bc", "post2")]
NORMS = ["pre1", "cq", "ckv", "qd0", "qd1", "kd", "post1", "pre2", "post2"]


def query_blocks(l):
    return list(range(CB if l == LAYERS - 1 else 0, NB))


def query_range(l, h, kb):
    t0 = CTX if l == LAYERS - 1 else 0
    if kb < CB:
        return t0, TOK
    if HEADS[h][0] != "A":
        return CTX, TOK
    j = kb - CB
    return CTX + P * max(j - 1, 0), CTX + P * min(j + 2, LAT // P)


def key_spans(h, b):
    if b < CB:
        return [(0, 0, CTX, [])]
    if HEADS[h][0] != "A":
        return [(0, 0, 512, []), (512, 512, TOK - 512, [])]
    first, end = max(b - 1, CB), min(b + 2, NB)
    spans = [(0, 0, CTX, [])]
    for j in range(first, end, 2):
        n = min(2, end - j)
        masks = [(CTX + (jj - first) * P, "before" if jj < b else "after") for jj in range(j, j + n) if jj != b]
        spans.append((CTX + (j - first) * P, j * P, n * P, masks))
    return spans


def keys_read(h, b):
    c0, _, n, _ = key_spans(h, b)[-1]
    return c0 + n


def product_order(l):
    qb = query_blocks(l)

    def alternate(keys):
        return [((k[0], l, *k[1:]), 2 + n % 2) for n, k in enumerate(keys)]

    order = ([(("ada", l), 3)] if l == 0 else []) + alternate(AUX) + [(("tile", l, i), i % 2) for i in range(N_IN)]
    order += [(("max", l, 0, b), 3) for b in qb] + [(("negm", l, 0), 3)]
    for h in range(NH):
        for j in range(len(KEYS)):
            order.append((("s", l, h, j), j % 2))
            if h + 1 < NH and 2 <= j < 5:
                order += [(("max", l, h + 1, b), 3) for b in qb[2 * (j - 2):2 * (j - 1)]]
        if h + 1 < NH:
            order.append((("negm", l, h + 1), 3))
        order.append((("o", l, h), 2))
        if h == 0:
            order += [(("pool", l, c), 3) for c in range(2)]
    order += [(("tile", l, N_IN + m), m % 2) for m in range(N_OUT)] + alternate(AUX2)
    order += [(("tile", l, N_IN + N_OUT + f), f % 4) for f in range(TILES - N_IN - N_OUT)]
    return order + alternate(AUX3)


def psum_plan():
    plan, uses, numbers = {}, [0] * 4, {}
    for l in range(LAYERS):
        for key, slot in product_order(l):
            plan[key] = (slot, uses[slot])
            uses[slot] += 1
            if key[0] not in ("tile", "o"):
                numbers[key] = len(numbers) + 1
    return plan, numbers


PLAN, AUXN = psum_plan()


def build(nc, x_t, cond, cond_t, ada_first, ada_t, stream, params, wuq_t, wukv_t, pool_w, consts, consts_b, rope_t, out_t):
    ctx = ExitStack()
    with ctx:
        def sem(name):
            return ctx.enter_context(nc.semaphore(name))

        used = [nc.sbuf_base + (-nc.sbuf_base) % 32]

        def sb(name, shape, dt=F32, at=None):
            size = 2 if dt == BF16 else 4
            for s in shape[1:]:
                size *= s
            here = used[0] if at is None else at
            if at is None:
                used[0] = here + size + (-size) % 32
            return nc.alloc_sbuf_tensor_at(name, shape, dt, offset=here)

        xT = sb("xT", [P, DC, TOK])
        h_hi = sb("h_hi", [P, DC, TOK], F32R)
        h_lo = sb("h_lo", [P, DC, TOK], F32R)
        w_raw = sb("w_raw", [P, 2, DC, P])
        w_hi = sb("w_hi", [P, 2, DC, P], F32R)
        w_lo = sb("w_lo", [P, 2, DC, P], F32R)
        work = sb("work", [P, 6, PW])
        par = sb("par", [P, LAYERS, NPAR])
        mod = sb("mod", [P, LAYERS * ADA, 2])
        coef = sb("coef", [P, LAYERS, 4, DC, 2])
        kf = sb("kf", [P, NCONST])
        kb16 = sb("kb16", [P, 4, P], BF16)
        negmax = sb("negmax", [P, NB])
        stat = sb("stat", [P, 2, 2 * NB])
        sink8 = sb("sink8", [P, LAYERS, 4])
        adacc = sb("adacc", [P, ADA_G, 2])
        silu_t = sb("silu_t", [P, DC, 2])
        eps = sb("eps", [P, 1])
        tick = sb("tick", [P, 2])
        phase = used[0]
        QK = sb("QK", [P, 20, TOK])
        V = sb("V", [P, NB, 8, P])
        wuq_at = used[0]
        wuq = sb("wuq", [P, 2, 384])
        cast_rows = sb("cast_rows", [P, 2, TOK], BF16, at=wuq_at)
        negm_diag = sb("negm_diag", [P, TOK], BF16)
        rope_tab = sb("rope_tab", [P, 4, LAT])
        wukv = sb("wukv", [P, 512])
        poolw = sb("poolw", [P, 2, P])
        assert used[0] <= nc.sbuf_usable_end, used[0]
        ada_w = sb("ada_w", [P, ADA_FIRST, DC, P], at=phase)
        used[0] = phase
        act_hi = sb("act_hi", [P, FG[0], TOK], F32R)
        act_lo = sb("act_lo", [P, FG[0], TOK], F32R)
        y = sb("y", [P, DC, TOK])
        assert used[0] <= nc.sbuf_usable_end
        ada_mid = sb("ada_mid", [P, MID_SLOTS, D], at=phase)
        ada1 = sb("ada1", [P, 2, D])
        cond1 = sb("cond1", [P, 2, D])
        assert used[0] <= nc.sbuf_usable_end, used[0]

        ps = [ctx.enter_context(nc.psum_tensor(f"ps{i}", [P, 1024], F32)) for i in range(4)]

        ident = kf[:, KID:KID + P]
        id16, upper16, lower16, ones16 = (kb16[:, i, :] for i in range(4))
        cos_hd, sin_hd = (rope_tab[:, RHD + i, :] for i in range(2))
        cos_c, sin_c = (rope_tab[64:96, RC + i, :] for i in range(2))

        consts_in, x_in, cond_in = sem("consts_in"), [sem("x_in0"), sem("x_in1")], sem("cond_in")
        lora_in = sem("lora_in")
        ada_first_in = [sem(f"ada_first_in{i}") for i in range(DC)]
        ada_mid_in = [sem(f"ada_mid_in{i}") for i in range(MID_SLOTS)]
        ada1_in = [sem("ada1_in0"), sem("ada1_in1")]
        raw_in = [sem("raw_in0"), sem("raw_in1")]
        silu_done = sem("silu_done")
        ada_used = sem("ada_used")
        coef_ready = sem("coef_ready")
        slot_free = sem("slot_free")
        hi_made, split_done = sem("hi_made"), sem("split_done")
        tile_done = sem("tile_done")
        aux_done = sem("aux_done")
        pv_done = sem("pv_done")
        read_out = [sem(f"read_out{i}") for i in range(4)]
        dve_step = sem("dve_step")
        act_step = sem("act_step")
        sq_ready, sum_step = sem("sq_ready"), sem("sum_step")
        rstd_ready, bcast_ready = sem("rstd_ready"), sem("bcast_ready")
        scaled, hi_ready, lo_ready = sem("scaled"), sem("hi_ready"), sem("lo_ready")
        swapped, roped = sem("swapped"), sem("roped")
        lowrank_ready = sem("lowrank_ready")
        krope_ready, krope_spread = sem("krope_ready"), sem("krope_spread")
        qc_roped = sem("qc_roped")
        v_ones = sem("v_ones")
        pads, pooled = sem("pads"), sem("pooled")
        pool_step = sem("pool_step")
        ypool_hi, ypool_f = sem("ypool_hi"), sem("ypool_f")
        ypool_done = sem("ypool_done")
        casts, max_done, diag_ready = sem("casts"), sem("max_done"), sem("diag_ready")
        o_used, head_done = sem("o_used"), sem("head_done")
        x_new = sem("x_new")
        prod_step = sem("prod_step")
        silu_free = sem("silu_free")
        ada_copied = sem("ada_copied")
        act_hi_made = sem("act_hi_made")
        out_done = sem("out_done")

        def filled(eng, key):
            if key[0] == "tile":
                eng.wait_ge(tile_done, key[1] * TILES + key[2] + 1)
            else:
                eng.wait_ge(aux_done, AUXN[key])

        def read(eng, key):
            slot, use = PLAN[key]
            eng.wait_ge(read_out[slot], use + 1)

        def pt(key):
            return ps[PLAN[key][0]]

        def reads(key):
            return read_out[PLAN[key][0]]

        def nid(l, name):
            return l * len(NORMS) + NORMS.index(name)

        def streams(t0):
            return [(slice(CTX, TOK), 0)] + ([(slice(0, CTX), 1)] if t0 == 0 else [])

        def t0_of(l, name):
            return CTX if l == LAYERS - 1 and name in ("qd0", "qd1", "cq", "post1", "pre2", "post2") else 0

        def heads_in(name):
            return 2 if name in ("qd0", "qd1", "kd") else 1

        def scratch(c):
            return work[:, c, 0:TOK]

        RAW = {"cq": [QK[:, 0, :], QK[:, 1, :]], "ckv": [QK[:, 2, :]],
               "qd0": [QK[:, 9, :]], "qd1": [QK[:, 11, :]], "kd": [QK[:, 19, :]]}
        SQ = {"cq": [0, 1], "ckv": [2], "qd0": [0], "qd1": [1], "kd": [2]}
        MEAN = {"pre1": 0, "post1": 0, "pre2": 0, "post2": 0, "cq": 1, "ckv": 2, "qd0": 3, "qd1": 3, "kd": 3}
        B_ROW = 3

        def sq_count(l, name, n):
            return (3 * l + ("pre1", "pre2", "post2").index(name)) * DC + n

        def rope_count(l, n):
            return 2 * (6 * l + n)

        def norm_scaled(l, name, n):
            per = [("pre1", DC), ("cq", 2), ("ckv", 1), ("qd0", 1), ("qd1", 1), ("kd", 1), ("pre2", DC)]
            total = l * sum(k for _, k in per)
            for who, k in per:
                if who == name:
                    return total + n
                total += k

        block = ctx.enter_context(nc.Block())

        @block.sync
        def _(sp):
            sp.dma_start(kf[:, :], consts).then_inc(consts_in, 16)
            sp.dma_start(kb16[:, :, :], consts_b).then_inc(consts_in, 16)
            sp.dma_start(par[:, :, :], params).then_inc(consts_in, 16)
            sp.dma_start(silu_t[:, :, :], cond_t).then_inc(cond_in, 16)
            for c in range(0, DC, 4):
                sp.dma_start(xT[:, c:c + 4, :], x_t[:, c:c + 4, :]).then_inc(x_in[c // 4], 16)
            for i in range(DC):
                sp.dma_start(ada_w[:, 2 * i:2 * i + 2, :, :], ada_first[:, 2 * i:2 * i + 2]).then_inc(ada_first_in[i], 16)

            def lowrank_weights(l):
                sp.dma_start(wuq[:, :, :], wuq_t[l]).then_inc(lora_in, 16)
                sp.dma_start(wukv[:, :], wukv_t[l]).then_inc(lora_in, 16)
                sp.dma_start(poolw[:, :, :], pool_w[l]).then_inc(lora_in, 16)
                sp.dma_start(rope_tab[:, :, :], rope_t).then_inc(lora_in, 16)

            for l in range(LAYERS):
                base = l * TILES
                if l == 0:
                    for n in range(2):
                        sp.dma_start(w_raw[:, n, :, :], stream[n]).then_inc(raw_in[n], 16)
                    lowrank_weights(0)
                with sp.Fori(0, TILES // 2 - 1) as i:
                    for n in range(2):
                        sp.wait_ge(split_done, i * 2 + (base + n + 1))
                        sp.dma_start(w_raw[:, n, :, :], stream[i * 2 + (base + n + 2)]).then_inc(raw_in[n], 16)
                if l + 1 < LAYERS:
                    for n in range(2):
                        sp.wait_ge(split_done, base + TILES - 1 + n)
                        sp.dma_start(w_raw[:, n, :, :], stream[base + TILES + n]).then_inc(raw_in[n], 16)
                    sp.wait_ge(tile_done, base + TILES)
                    sp.wait_ge(x_new, (2 * l + 2) * DC)
                    sp.wait_ge(ada_used, 2 * (LAYERS * ADA - ADA_FIRST))
                    lowrank_weights(l + 1)
            sp.wait_ge(x_new, 2 * LAYERS * DC)
            sp.dma_start(out_t, xT[:, :, CTX:TOK]).then_inc(out_done, 16)
            sp.wait_ge(out_done, 16)

        @block.gpsimd
        def _(pool):
            def split(n, slot, round_, used_tiles):
                pool.wait_ge(raw_in[slot], round_)
                if used_tiles is not None:
                    pool.wait_ge(tile_done, used_tiles)
                    pool.wait_ge(slot_free, n - 1)
                    nc.gpsimd.tensor_tensor(tick[:, 1:2], tick[:, 0:1], tick[:, 0:1],
                                            ALU.add).then_inc(slot_free, 1)
                nc.gpsimd.tensor_scalar(w_hi[:, slot, :, :], w_raw[:, slot, :, :], 0.0, 1.0,
                                        ALU.add, ALU.mult).then_inc(hi_made, 1)
                pool.wait_ge(hi_made, n + 1)
                nc.gpsimd.tensor_tensor(w_lo[:, slot, :, :], w_raw[:, slot, :, :],
                                        w_hi[:, slot, :, :].bitcast(F32), ALU.subtract).then_inc(split_done, 1)

            def link(ins):
                steps[0] += 1
                ins.then_inc(pool_step, 1)
                pool.wait_ge(pool_step, steps[0])

            def windows(l):
                a, b = work[:, 4, :], work[:, 5, :]
                for c in range(2):
                    u = work[:, 3, :] if c == 0 else work[:, 2, :]
                    pool.wait_ge(pads, 2 * l + c + 1)
                    read(pool, ("tile", l, UB0 + c))
                    if c == 1:
                        pool.wait_ge(ypool_f, 2 * l + 1)
                    lo, hi = 0, PW
                    rows = slice(0, P)
                    prev, cur = u, a
                    for s, (left, right) in enumerate([(-1, 0), (-1, 1), (-2, 2), (-4, 4)][:2 * c + 2]):
                        lo, hi = lo - left, hi - right
                        if s == 2 * c + 1:
                            link(nc.gpsimd.tensor_copy(cur[0:64, lo:hi], prev[0:64, lo:hi]))
                            rows = slice(64, P)
                        link(nc.gpsimd.tensor_tensor(cur[rows, lo:hi], prev[rows, lo + left:hi + left],
                                                     prev[rows, lo + right:hi + right], ALU.add))
                        prev, cur = cur, (b if cur is a else a)
                    nc.gpsimd.nop().then_inc(pooled, 1)

            nc.gpsimd.memset(tick[:, :], 0.0).then_inc(slot_free, 1)
            steps = [0]
            for n in range(2):
                split(n, n, 16, None)
            for l in range(LAYERS):
                base = l * TILES
                start = 2 if l == 0 else 0
                with pool.Fori(start // 2, (N_IN + 2) // 2) as i:
                    for n in range(2):
                        split(i * 2 + (base + n), n, i * 16 + 16 * (base // 2 + 1), i * 2 + (base + n - 1))
                windows(l)
                with pool.Fori((N_IN + 2) // 2, TILES // 2) as i:
                    for n in range(2):
                        split(i * 2 + (base + n), n, i * 16 + 16 * (base // 2 + 1), i * 2 + (base + n - 1))

        @block.scalar
        def _(act):
            steps = [0]
            sums = [0]
            squares = [0]

            def link(ins):
                steps[0] += 1
                ins.then_inc(act_step, 1)
                act.wait_ge(act_step, steps[0])

            def act_square(out, in_):
                nc.scalar.activation(out, in_, ACT.Square).then_inc(sq_ready, 1)

            def squares_of(l, name, src, ready):
                t0 = t0_of(l, name)
                for c in range(DC):
                    ready(c)
                    if c == 0:
                        if squares[0]:
                            act.wait_ge(aux_done, last_sum[0])
                        dst = work[:, 2, t0:TOK]
                    else:
                        if c > 2:
                            act.wait_ge(sum_step, sums[0] + c - 2)
                        dst = work[:, c % 2, t0:TOK]
                    act_square(dst, src[:, c, t0:TOK])
                    squares[0] += 1
                sums[0] += DC - 1
                last_sum[0] = AUXN[("sum", l, name)]

            last_sum = [0]

            def rms(l, name):
                key = ("sum", l, name)
                nh = heads_in(name)
                b0 = t0_of(l, name) // P
                filled(act, key)
                nc.scalar.activation(stat[:, 0, b0 * nh:NB * nh], pt(key)[:, b0 * nh:NB * nh], ACT.Sqrt,
                                     bias=eps[:, 0:1]).then_inc(reads(key), 1)
                act.wait_ge(rstd_ready, nid(l, name) + 1)
                if nid(l, name):
                    act.wait_ge(aux_done, last_bc[0])
                last_bc[0] = AUXN[("bc", l, name)]
                nc.scalar.activation(
                    work[:, B_ROW, b0 * P:TOK].rearrange("p (b c) -> p b c", c=P // nh),
                    stat[:, 1, b0 * nh:NB * nh].unsqueeze(2).broadcast_to([P, (NB - b0) * nh, P // nh]),
                    ACT.Copy).then_inc(bcast_ready, 1)

            last_bc = [0]

            def shifts(l, name, which):
                t0 = t0_of(l, name)
                norm = 2 * l + (name == "pre2")
                for c in range(DC):
                    act.wait_ge(scaled, norm_scaled(l, name, c + 1))
                    for cols, s in streams(t0):
                        nc.scalar.activation(h_hi[:, c, cols], work[:, 4 + c % 2, cols], ACT.Identity,
                                             bias=mod[:, l * ADA + which * DC + c, s:s + 1]).then_inc(hi_ready, 1)

            def raw_and_square(l, i, name, c):
                key = ("tile", l, i)
                t0 = t0_of(l, name)
                n = TOK - t0
                filled(act, key)
                nc.scalar.activation(RAW[name][c][:, t0:TOK], pt(key)[:, 0:n], ACT.Copy).then_inc(act_step, 1)
                steps[0] += 1
                nc.scalar.activation(scratch(SQ[name][c])[:, t0:TOK], pt(key)[:, 0:n],
                                     ACT.Square).then_inc(reads(key), 1)

            ropes = [0]

            def swap_halves(src, dst_even, dst_odd, off, has_ctx, ready):
                ready()
                if has_ctx:
                    for q, dst in ((0, dst_even), (64, dst_odd)):
                        nc.scalar.activation(dst[0:64, 0:CTX], src[q:q + 64, 0:CTX],
                                             ACT.Copy).then_inc(swapped, 1)
                if ropes[0]:
                    act.wait_ge(roped, ropes[0])
                ropes[0] += 2
                for q in range(4):
                    nc.scalar.activation(work[32 * (q ^ 1):32 * (q ^ 1) + 32, 4, 0:LAT],
                                         src[32 * q:32 * q + 32, off:off + LAT], ACT.Copy).then_inc(swapped, 1)

            act.wait_ge(cond_in, 16)
            nc.scalar.activation(silu_t[:, :, :], silu_t[:, :, :], ACT.Silu).then_inc(silu_done, 1)

            for l in range(LAYERS):
                last = l == LAYERS - 1
                if l == 0:
                    squares_of(l, "pre1", xT, lambda c: act.wait_ge(x_in[c // 4], 16))
                else:
                    squares_of(l, "pre1", xT, lambda c: act.wait_ge(x_new, (2 * l - 1) * DC + c + 1))
                rms(l, "pre1")
                shifts(l, "pre1", 0)

                for i, b0, b1 in ((VA, 0, 4), (VD, 4, NB)):
                    key = ("tile", l, i)
                    filled(act, key)
                    nc.scalar.activation(
                        V[:, b0:b1, 0:4, 0:64],
                        pt(key)[:, 0:256 * (b1 - b0)].rearrange("p (b h d) -> p b h d", h=4, d=64),
                        ACT.Copy).then_inc(reads(key), 1)
                if l:
                    act.wait_ge(aux_done, AUXN[("sum", l, "pre1")])
                raw_and_square(l, CQ0, "cq", 0)
                raw_and_square(l, CQ1, "cq", 1)
                raw_and_square(l, CKV, "ckv", 0)
                rms(l, "cq")
                key = ("tile", l, KR)
                filled(act, key)
                nc.scalar.activation(QK[64:96, 14, :], pt(key)[0:32, 0:TOK], ACT.Copy).then_inc(reads(key), 1)
                rms(l, "ckv")
                act.wait_ge(aux_done, AUXN[("sum", l, "cq")])
                raw_and_square(l, QD0, "qd0", 0)
                for h in range(3):
                    act.wait_ge(krope_ready, l + 1)
                    nc.scalar.activation(QK[64:96, 15 + h, :], QK[64:96, 14, :], ACT.Copy).then_inc(krope_spread, 1)
                raw_and_square(l, QD1, "qd1", 0)
                rms(l, "qd0")
                tq = CTX if last else 0
                for h in range(4):
                    key = ("lq", l, h)
                    filled(act, key)
                    nc.scalar.activation(QK[0:96, 4 + h, tq:TOK], pt(key)[0:96, 0:TOK - tq],
                                         ACT.Copy).then_inc(reads(key), 1)
                act.wait_ge(aux_done, AUXN[("sum", l, "ckv")])
                raw_and_square(l, KD, "kd", 0)
                swap_halves(QK[:, 9, :], QK[:, 8, :], QK[:, 9, :], CTX, False,
                            lambda: act.wait_ge(scaled, norm_scaled(l, "qd0", 1)))
                rms(l, "qd1")
                for h in range(4):
                    key = ("lk", l, h)
                    filled(act, key)
                    nc.scalar.activation(QK[0:64, 14 + h, :], pt(key)[0:64, 0:TOK],
                                         ACT.Copy).then_inc(reads(key), 1)
                for c in range(2):
                    key = ("lv", l, c)
                    filled(act, key)
                    b0, b1 = (0, 4) if c == 0 else (4, NB)
                    nc.scalar.activation(
                        V[:, b0:b1, 4:8, 0:64],
                        pt(key)[:, 0:256 * (b1 - b0)].rearrange("p (b h d) -> p b h d", h=4, d=64),
                        ACT.Copy).then_inc(reads(key), 1)
                swap_halves(QK[:, 11, :], QK[:, 10, :], QK[:, 11, :], CTX, False,
                            lambda: act.wait_ge(scaled, norm_scaled(l, "qd1", 1)))
                rms(l, "kd")
                swap_halves(QK[:, 19, :], QK[:, 18, :], QK[:, 19, :], CTX, False,
                            lambda: act.wait_ge(scaled, norm_scaled(l, "kd", 1)))
                for i, even in ((QA0, 0), (QA1, 2), (KA, 12)):
                    key = ("tile", l, i)
                    src = pt(key)
                    off = 0 if last and i != KA else CTX
                    if i == QA0:
                        act.wait_ge(aux_done, AUXN[("lv", l, 1)])
                    swap_halves(src, QK[:, even, :], QK[:, even + 1, :], off, off == CTX,
                                lambda: filled(act, key))
                for c in range(2):
                    key = ("tile", l, UB0 + c)
                    dst = work[:, 3 if c == 0 else 2, :]
                    filled(act, key)
                    if c == 0:
                        act.wait_ge(aux_done, AUXN[("bc", l, "kd")])
                    act.wait_ge(pads, 2 * l + c + 1)
                    link(nc.scalar.activation(dst[:, PAD:PAD + CTX], pt(key)[:, 0:CTX], ACT.Copy))
                    nc.scalar.activation(dst[:, 3 * PAD + CTX:3 * PAD + TOK], pt(key)[:, CTX:TOK],
                                         ACT.Copy).then_inc(reads(key), 1)

                n_q = TOK - tq

                def negmax_row(h):
                    kind, q, _, _, rows, _ = HEADS[h]
                    key = ("negm", l, h)
                    filled(act, key)
                    ins = nc.scalar.activation(QK[rows:rows + 1, q, tq:TOK], pt(key)[rows:rows + 1, 0:n_q], ACT.Copy)
                    if kind == "A":
                        link(ins)
                        act.wait_ge(o_used, l * NH + h - 1)
                        ins = nc.scalar.activation(work[64:P, 2 + h % 2, 0:n_q], pt(key)[64:P, 0:n_q], ACT.Exp,
                                                   bias=par[64:P, l, PSINK + h - (NH - 4):PSINK + h - (NH - 4) + 1],
                                                   scale=SCALE[kind])
                    ins.then_inc(reads(key), 1)

                negmax_row(0)
                for h in range(NH):
                    kind = HEADS[h][0]
                    for j, kb in enumerate(KEYS):
                        u = (l * NH + h) * len(KEYS) + j
                        key = ("s", l, h, j)
                        a, b = query_range(l, h, kb)
                        filled(act, key)
                        if u >= 2:
                            act.wait_ge(pv_done, u - 1)
                        nc.scalar.activation(work[:, j % 2, a:b], pt(key)[:, a - tq:b - tq], ACT.Exp,
                                             scale=SCALE[kind]).then_inc(reads(key), 1)
                    if h + 1 < NH:
                        negmax_row(h + 1)
                    act.wait_ge(pv_done, (l * NH + h + 1) * len(KEYS))
                    if h:
                        act.wait_ge(o_used, l * NH + h)
                    if h == 0:
                        act.wait_ge(ypool_f, 2 * l + 2)
                    nc.scalar.activation(work[:, 4, 0:n_q], pt(("o", l, h))[:, 0:n_q],
                                         ACT.Copy).then_inc(read_out[2], 1)

                t0 = tq
                act.wait_ge(head_done, (l + 1) * NH)
                if l == 0:
                    act.dma_start(cond1[:, :, :], cond.partition_broadcast(P)).then_inc(cond_in, 16)
                    for n in range(MID_SLOTS):
                        act.dma_start(ada_mid[:, n, :], ada_t[n]).then_inc(ada_mid_in[n], 16)
                    for m in range(2):
                        act.dma_start(ada1[:, m, :], ada_t[ADA_MID + m]).then_inc(ada1_in[m], 16)
                    act.wait_ge(cond_in, 32)
                    nc.scalar.activation(cond1[:, :, :], cond1[:, :, :], ACT.Silu).then_inc(silu_done, 1)
                for c in range(DC):
                    key = ("tile", l, N_IN + c)
                    if l == 0:
                        for n in range(MID_SLOTS + 3 * (c - 1), min(MID_SLOTS + 3 * c, ADA_MID)):
                            if n >= MID_SLOTS:
                                act.wait_ge(ada_used, 2 * (n - MID_SLOTS + 1))
                                act.dma_start(ada_mid[:, n % MID_SLOTS, :], ada_t[n]
                                              ).then_inc(ada_mid_in[n % MID_SLOTS], 16)
                    filled(act, key)
                    link(nc.scalar.activation(y[:, c, t0:TOK], pt(key)[:, 0:n_q], ACT.Copy))
                    if c > 2:
                        act.wait_ge(sum_step, sums[0] + c - 2)
                    dst = work[:, 2, t0:TOK] if c == 0 else work[:, c % 2, t0:TOK]
                    nc.scalar.activation(dst, pt(key)[:, 0:n_q], ACT.Square).then_inc(reads(key), 1)
                sums[0] += DC - 1
                last_sum[0] = AUXN[("sum", l, "post1")]
                rms(l, "post1")
                squares_of(l, "pre2", xT, lambda c: act.wait_ge(x_new, 2 * l * DC + c + 1))
                rms(l, "pre2")
                shifts(l, "pre2", 3)
                def ada_load(first, i, m):
                    act.wait_ge(ada_used, i * (2 * ADA_G) + 2 * (ADA_MID + ADA_G * first + m + 1))
                    act.dma_start(ada1[:, m % 2, :], ada_t[i * ADA_G + (ADA_MID + ADA_G * first + m + 2)]
                                  ).then_inc(ada1_in[m % 2], 16)

                pairs = 0
                groups = 0
                f0 = N_IN + N_OUT
                for g, ng in enumerate(FG):
                    with act.Fori(0, ng // 2) as i:
                        for e in range(2):
                            if l == 0:
                                for m in (2 * e, 2 * e + 1):
                                    ada_load(groups, i, m)
                            act.wait_ge(tile_done, i * 4 + (l * TILES + f0 + 2 * e + 1))
                            act.wait_ge(silu_free, i * 2 + (l * sum(FG) + pairs + e + 1))
                            nc.scalar.activation(work[:, e, t0:TOK], ps[2 * e][:, 0:n_q],
                                                 ACT.Silu).then_inc(read_out[2 * e], 1)
                    pairs += ng
                    groups += ng // 2
                    f0 += 2 * ng
                    if g == 0:
                        with act.Fori(0, DC // 4) as i:
                            for m in range(4):
                                if l == 0:
                                    ada_load(groups, i, m)
                                act.wait_ge(tile_done, i * 4 + (l * TILES + f0 + m + 1))
                                nc.scalar.activation(y[:, bass.ds(i * 4 + m, 1), t0:TOK],
                                                     ps[m][:, 0:n_q].unsqueeze(1), ACT.Copy).then_inc(read_out[m], 1)
                        groups += DC // 4
                    if l == 0 and g == len(FG) - 1:
                        for m in range(2):
                            ada_load(groups, 0, m)
                    f0 += DC
                squares_of(l, "post2", y, lambda c: read(act, ("tile", l, TILES - DC + c)))
                rms(l, "post2")

        @block.vector
        def _(dve):
            steps = [0]
            sums = [0]
            his = [0]
            swaps = [0]
            los = [0]
            xs = [0]

            def link(ins):
                steps[0] += 1
                ins.then_inc(dve_step, 1)
                dve.wait_ge(dve_step, steps[0])

            def add_squares(l, name, ready):
                t0 = t0_of(l, name)
                total = work[:, 2, t0:TOK]
                for c in range(1, DC):
                    ready(c)
                    if c > 1:
                        dve.wait_ge(sum_step, sums[0])
                    nc.vector.tensor_tensor(total, total, work[:, c % 2, t0:TOK], ALU.add).then_inc(sum_step, 1)
                    sums[0] += 1

            def reciprocal(l, name):
                nh = heads_in(name)
                b0 = t0_of(l, name) // P
                read(dve, ("sum", l, name))
                nc.vector.reciprocal(stat[:, 1, b0 * nh:NB * nh],
                                     stat[:, 0, b0 * nh:NB * nh]).then_inc(rstd_ready, 1)

            def modulate(l, name, which):
                t0 = t0_of(l, name)
                key = ("bc", l, name)
                filled(dve, key)
                n_s = len(streams(t0))

                def low(c):
                    dve.wait_ge(hi_ready, his[0] + n_s)
                    his[0] += n_s
                    for cols, s in streams(t0):
                        nc.vector.scalar_tensor_tensor(
                            out=h_lo[:, c, cols], in0=work[:, 4 + c % 2, cols],
                            scalar=mod[:, l * ADA + which * DC + c, s:s + 1], in1=h_hi[:, c, cols].bitcast(F32),
                            op0=ALU.add, op1=ALU.subtract).then_inc(lo_ready, 1)
                        los[0] += 1

                for c in range(DC):
                    if c >= 2:
                        low(c - 2)
                        dve.wait_ge(lo_ready, los[0])
                    for n, (cols, s) in enumerate(streams(t0)):
                        ins = nc.vector.scalar_tensor_tensor(
                            out=work[:, 4 + c % 2, cols], in0=xT[:, c, cols],
                            scalar=coef[:, l, 0 if name == "pre1" else 2, c, s:s + 1],
                            in1=pt(key)[:, cols.start - t0:cols.stop - t0], op0=ALU.mult, op1=ALU.mult)
                        if n + 1 < n_s:
                            ins.then_inc(dve_step, 1)
                            steps[0] += 1
                    ins.then_inc(scaled, 1)
                low(DC - 2)
                low(DC - 1)
                dve.wait_ge(lo_ready, los[0])

            def residual(l, name, which, src):
                t0 = t0_of(l, name)
                key = ("bc", l, name)
                filled(dve, key)
                for c in range(DC):
                    if c >= 2:
                        dve.wait_ge(x_new, xs[0] - 1)
                    for n, (cols, s) in enumerate(streams(t0)):
                        ins = nc.vector.scalar_tensor_tensor(
                            out=work[:, 4 + c % 2, cols], in0=src[:, c, cols],
                            scalar=coef[:, l, which, c, s:s + 1],
                            in1=pt(key)[:, cols.start - t0:cols.stop - t0], op0=ALU.mult, op1=ALU.mult)
                        steps[0] += 1
                        ins.then_inc(dve_step, 1)
                    dve.wait_ge(dve_step, steps[0])
                    nc.vector.tensor_tensor(xT[:, c, t0:TOK], xT[:, c, t0:TOK], work[:, 4 + c % 2, t0:TOK],
                                            ALU.add).then_inc(x_new, 1)
                    xs[0] += 1
                dve.wait_ge(x_new, xs[0])
                release(key)

            def release(key):
                dve.wait_ge(dve_step, steps[0])
                dve.nop().then_inc(reads(key), 1)

            def apply_norm(l, name, gain):
                t0 = t0_of(l, name)
                key = ("bc", l, name)
                filled(dve, key)
                for c, raw in enumerate(RAW[name]):
                    nc.vector.scalar_tensor_tensor(
                        out=raw[:, t0:TOK], in0=raw[:, t0:TOK], scalar=par[:, l, gain + c:gain + c + 1],
                        in1=pt(key)[:, 0:TOK - t0], op0=ALU.mult, op1=ALU.mult).then_inc(scaled, 1)
                dve.wait_ge(scaled, norm_scaled(l, name, len(RAW[name])))
                dve.nop().then_inc(reads(key), 1)

            def rope(src, dst_even, dst_odd, off, has_ctx, key=None):
                swaps[0] += 4 + 2 * has_ctx
                dve.wait_ge(swapped, swaps[0])
                t1, t2 = work[:, 5, 0:LAT], work[:, 4, 0:LAT]
                ins = nc.vector.tensor_tensor(t1, src[:, off:off + LAT], cos_hd, ALU.mult)
                link(ins)
                if key is not None:
                    dve.nop().then_inc(reads(key), 1)
                link(nc.vector.tensor_tensor(t2, t2, sin_hd, ALU.mult))
                if key is None:
                    for q, dst in ((0, dst_even), (64, dst_odd)):
                        if src_ctx[0]:
                            link(nc.vector.tensor_copy(dst[0:64, 0:CTX], src[q:q + 64, 0:CTX]))
                for q, dst in ((0, dst_even), (64, dst_odd)):
                    nc.vector.tensor_tensor(dst[0:64, CTX:TOK], work[q:q + 64, 5, 0:LAT],
                                            work[q:q + 64, 4, 0:LAT], ALU.add).then_inc(roped, 1)

            src_ctx = [True]

            def rope_c(tile):
                x = QK[64:96, tile, CTX:TOK]
                t1, t2 = work[64:96, 5, 0:LAT], work[64:96, 4, 0:LAT]
                link(nc.vector.stream_shuffle(t2, x, list(range(16, 32)) + list(range(16))))
                link(nc.vector.tensor_tensor(t1, x, cos_c, ALU.mult))
                link(nc.vector.tensor_tensor(t2, t2, sin_c, ALU.mult))
                return nc.vector.tensor_tensor(x, t1, t2, ALU.add)

            def add_bias(l, first, end, values=None):
                m = mod[:, l * ADA + first:l * ADA + end, :]
                b = par[:, l, PB_ADA + first:PB_ADA + end].unsqueeze(2).broadcast_to([P, end - first, 2])
                link(nc.vector.tensor_tensor(m, m if values is None else values, b, ALU.add))

            coefs = [0]

            def coefficients(l, norms):
                for n in norms:
                    vec, plus = ((1, 1.0), (2, 0.0), (4, 1.0), (5, 0.0))[n]
                    g = par[:, l, n * DC:(n + 1) * DC].unsqueeze(2).broadcast_to([P, DC, 2])
                    at = l * ADA + vec * DC
                    nc.vector.scalar_tensor_tensor(out=coef[:, l, n, :, :], in0=mod[:, at:at + DC, :],
                                                   scalar=plus, in1=g, op0=ALU.add, op1=ALU.mult
                                                   ).then_inc(coef_ready, 1)
                    coefs[0] += 1
                dve.wait_ge(coef_ready, coefs[0])

            scrap = work[:, 4:6, :].rearrange("p a b -> p (a b)")[:, 0:D]

            def dot(weights, s, out, after):
                if after is not None:
                    dve.wait_ge(ada_used, after)
                nc.vector.tensor_tensor_reduce(weights if s else scrap, weights, cond1[:, s, :], 1.0, 0.0,
                                               ALU.mult, ALU.add, out).then_inc(ada_used, 1)

            link(nc.vector.memset(eps[:, :], EPS))
            dve.nop().then_inc(silu_free, 1)
            dve.nop().then_inc(silu_free, 1)
            dve.wait_ge(consts_in, 48)
            link(nc.vector.tensor_scalar(sink8[:, :, :], par[:, :, PSINK:PSINK + 4], -1.0 / SCALE["A"], None, ALU.mult))

            for l in range(LAYERS):
                last = l == LAYERS - 1
                tq = CTX if last else 0
                n_q = TOK - tq
                add_squares(l, "pre1", lambda c: dve.wait_ge(sq_ready, sq_count(l, "pre1", c + 1)))
                reciprocal(l, "pre1")
                if l == 0:
                    key = ("ada", 0)
                    filled(dve, key)
                    add_bias(0, 0, ADA_FIRST, pt(key)[:, 0:2 * ADA_FIRST].rearrange("p (m s) -> p m s", s=2))
                    dve.nop().then_inc(reads(key), 1)
                    coefficients(0, [0])
                modulate(l, "pre1", 0)
                release(("bc", l, "pre1"))
                nc.vector.memset(V[:, :, :, 64:P], 1.0).then_inc(v_ones, 1)
                nc.vector.memset(QK[64:65, 12:14, :], 1.0).then_inc(v_ones, 1)
                nc.vector.memset(QK[64:65, 18, :], 1.0).then_inc(v_ones, 1)
                nc.vector.memset(QK[96:97, 14:18, :], 1.0).then_inc(v_ones, 1)
                dve.wait_ge(v_ones, 5 * l + 4)
                dve.wait_ge(lora_in, 16 * 4 * (l + 1))
                reciprocal(l, "cq")
                reciprocal(l, "ckv")
                apply_norm(l, "cq", PGQ)
                read(dve, ("tile", l, KR))
                rope_c(14).then_inc(krope_ready, 1)
                apply_norm(l, "ckv", PGKV)
                reciprocal(l, "qd0")
                for h in range(4):
                    read(dve, ("lq", l, h))
                    if h == 0:
                        dve.wait_ge(krope_ready, l + 1)
                    else:
                        dve.wait_ge(qc_roped, 4 * l + h)
                    rope_c(4 + h).then_inc(qc_roped, 1)
                dve.wait_ge(qc_roped, 4 * l + 4)
                apply_norm(l, "qd0", PDGQ)
                src_ctx[0] = not last
                rope(QK[:, 9, :], QK[:, 8, :], QK[:, 9, :], CTX, False)
                reciprocal(l, "qd1")
                apply_norm(l, "qd1", PDGQ)
                dve.wait_ge(roped, rope_count(l, 1))
                rope(QK[:, 11, :], QK[:, 10, :], QK[:, 11, :], CTX, False)
                reciprocal(l, "kd")
                apply_norm(l, "kd", PDGK)
                src_ctx[0] = True
                dve.wait_ge(roped, rope_count(l, 2))
                rope(QK[:, 19, :], QK[:, 18, :], QK[:, 19, :], CTX, False)
                for n, (i, even) in enumerate(((QA0, 0), (QA1, 2), (KA, 12))):
                    key = ("tile", l, i)
                    off = 0 if last and i != KA else CTX
                    dve.wait_ge(roped, rope_count(l, 3 + n))
                    rope(pt(key), QK[:, even, :], QK[:, even + 1, :], off, off == CTX, key)
                dve.wait_ge(roped, rope_count(l, 6))
                nc.vector.memset(QK[64:65, 19, :], 1.0).then_inc(v_ones, 1)
                for c in range(2):
                    u = work[:, 3 if c == 0 else 2, :]
                    dve.wait_ge(aux_done, AUXN[("bc", l, "kd")])
                    link(nc.vector.memset(u[:, 0:PAD], 0.0))
                    link(nc.vector.memset(u[:, PAD + CTX:3 * PAD + CTX], 0.0))
                    nc.vector.memset(u[:, PW - PAD:PW], 0.0).then_inc(pads, 1)

                def cast(h):
                    _, q, k, _, rows, _ = HEADS[h]
                    if h:
                        dve.wait_ge(aux_done, AUXN[("max", l, h - 1, NB - 1)])
                    nc.vector.tensor_copy(cast_q[0:rows, tq:TOK], QK[0:rows, q, tq:TOK]).then_inc(casts, 1)
                    nc.vector.tensor_copy(cast_k[0:rows, :], QK[0:rows, k, :]).then_inc(casts, 1)

                def maxima(h):
                    kind = HEADS[h][0]
                    if l or h:
                        dve.wait_ge(diag_ready, l * NH + h)
                    for b in query_blocks(l):
                        key = ("max", l, h, b)
                        filled(dve, key)
                        nc.vector.tensor_reduce(negmax[:, b:b + 1], pt(key)[:, 0:keys_read(h, b)], AX.X, ALU.max,
                                                negate=True).then_inc(reads(key), 1)
                    read(dve, key)
                    b0 = tq // P
                    if kind == "A":
                        s = h - (NH - 4)
                        link(nc.vector.tensor_scalar(negmax[:, b0:NB], negmax[:, b0:NB], sink8[:, l, s:s + 1], None,
                                                     ALU.min))
                    if h:
                        filled(dve, ("negm", l, h - 1))
                    nc.vector.tensor_tensor(
                        negm_diag[:, tq:TOK].rearrange("p (b c) -> p b c", c=P),
                        id16.unsqueeze(1).broadcast_to([P, NB - b0, P]),
                        negmax[:, b0:NB].unsqueeze(2).broadcast_to([P, NB - b0, P]), ALU.mult).then_inc(diag_ready, 1)

                def finish(h):
                    kind, _, _, _, _, chunk = HEADS[h]
                    c, q = chunk // 2, 64 * (chunk % 2)
                    read(dve, ("o", l, h))
                    den = work[64:P, 4, 0:n_q]
                    if kind == "A":
                        link(nc.vector.tensor_tensor(den, den, work[64:P, 2 + h % 2, 0:n_q], ALU.add))
                    inv = work[0:64, 5, 0:n_q]
                    link(nc.vector.reciprocal(inv, den))
                    o = work[q:q + 64, 5, 0:n_q]
                    nc.vector.tensor_tensor(o, work[0:64, 4, 0:n_q], inv, ALU.mult).then_inc(o_used, 1)
                    dve.wait_ge(o_used, l * NH + h + 1)
                    link(nc.vector.tensor_copy(h_hi[q:q + 64, c, tq:TOK], o))
                    nc.vector.tensor_tensor(h_lo[q:q + 64, c, tq:TOK], o, h_hi[q:q + 64, c, tq:TOK].bitcast(F32),
                                            ALU.subtract).then_inc(head_done, 1)
                    dve.wait_ge(head_done, l * NH + h + 1)

                cast_q = cast_rows[:, 0, :]
                cast_k = cast_rows[:, 1, :]
                read(dve, ("lk", l, 3))
                dve.wait_ge(krope_spread, 3 * (l + 1))
                cast(0)
                maxima(0)
                cast(1)
                for c in range(2):
                    u = work[:, 3 if c == 0 else 2, :]
                    dve.wait_ge(pooled, 2 * l + c + 1)
                    s = work[:, 5, :]
                    for e, at in enumerate((PAD, CTX, 3 * PAD + CTX, 2 * PAD + TOK)):
                        k = KEDGE + (c * 4 + e) * PAD
                        link(nc.vector.tensor_tensor(s[:, at:at + PAD], s[:, at:at + PAD], kf[:, k:k + PAD], ALU.mult))
                    ins = nc.vector.scalar_tensor_tensor(
                        out=u[:, PAD:PW - PAD], in0=s[:, PAD:PW - PAD], scalar=kf[:, KINV + c:KINV + c + 1],
                        in1=u[:, PAD:PW - PAD], op0=ALU.mult, op1=ALU.subtract)
                    ins.then_inc(ypool_f, 1)
                for h in range(NH):
                    if h + 1 < NH:
                        maxima(h + 1)
                    if h + 2 < NH:
                        cast(h + 2)
                    if h == 0:
                        for c in range(2):
                            key = ("pool", l, c)
                            filled(dve, key)
                            f = work[:, 3, 0:n_q]
                            link(nc.vector.tensor_scalar(f, pt(key)[:, 0:n_q], par[:, l, PPS + c:PPS + c + 1], None,
                                                         ALU.mult))
                            dve.nop().then_inc(reads(key), 1)
                            link(nc.vector.tensor_copy(h_hi[:, 2 + c, tq:TOK], f))
                            link(nc.vector.tensor_tensor(h_lo[:, 2 + c, tq:TOK], f,
                                                         h_hi[:, 2 + c, tq:TOK].bitcast(F32), ALU.subtract))
                    finish(h)

                def square_ready(c):
                    if l == 0:
                        if c == 1:
                            dve.wait_ge(silu_done, 2)
                            mid_dots(0)
                        mid_dots(c)
                    read(dve, ("tile", l, N_IN + c))

                def mid_dots(c):
                    for n in range(3 * c, 3 * c + 3):
                        dve.wait_ge(ada_mid_in[n % MID_SLOTS], 16 * (n // MID_SLOTS + 1))
                        for s in range(2):
                            dot(ada_mid[:, n % MID_SLOTS, :], s, mod[:, ADA_FIRST + n, s:s + 1], 2 * n + s or None)

                add_squares(l, "post1", square_ready)
                if l == 0:
                    dve.wait_ge(ada_used, 2 * ADA_MID)
                    add_bias(0, ADA_FIRST, ADA_FIRST + ADA_MID)
                    coefficients(0, [1, 2])
                reciprocal(l, "post1")
                residual(l, "post1", 1, y)
                add_squares(l, "pre2", lambda c: dve.wait_ge(sq_ready, sq_count(l, "pre2", c + 1)))
                reciprocal(l, "pre2")
                modulate(l, "pre2", 3)
                release(("bc", l, "pre2"))

                pairs = 0
                f0 = N_IN + N_OUT
                groups = 0

                def ada_group(first, i):
                    for m in range(ADA_G):
                        dve.wait_ge(ada1_in[m % 2], i * 32 + (32 * first + 16 * (m // 2) + 16))
                        for s in range(2):
                            dot(ada1[:, m % 2, :], s, adacc[:, m, s:s + 1],
                                i * (2 * ADA_G) + (2 * (ADA_MID + ADA_G * first + m) + s))
                    dve.wait_ge(ada_used, i * (2 * ADA_G) + 2 * (ADA_MID + ADA_G * (first + 1)))
                    dst = mod[:, bass.ds(i * ADA_G + (ADA_FIRST + ADA_MID + first * ADA_G), ADA_G), :]
                    nc.vector.tensor_copy(dst, adacc[:, :, :]).then_inc(ada_copied, 1)
                    dve.wait_ge(ada_copied, i + (first + 1))

                for g, ng in enumerate(FG):
                    with dve.Fori(0, ng // 2) as i:
                        if l == 0:
                            ada_group(groups, i)
                        for e in range(2):
                            dve.wait_ge(tile_done, i * 4 + (l * TILES + f0 + 2 * e + 2))
                            dve.wait_ge(read_out[2 * e], i + (PLAN[("tile", l, f0 + 2 * e)][1] + 1))
                            prod = work[:, 2 + e, tq:TOK]
                            nc.vector.tensor_tensor(prod, work[:, e, tq:TOK], ps[2 * e + 1][:, 0:n_q],
                                                    ALU.mult).then_inc(read_out[2 * e + 1], 1)
                            dve.wait_ge(read_out[2 * e + 1], i + (PLAN[("tile", l, f0 + 2 * e + 1)][1] + 1))
                            at = bass.ds(i * 2 + e, 1)
                            nc.vector.tensor_copy(act_hi[:, at, tq:TOK], prod.unsqueeze(1)).then_inc(act_hi_made, 1)
                            dve.nop().then_inc(silu_free, 1)
                            dve.wait_ge(act_hi_made, i * 2 + (l * sum(FG) + pairs + e + 1))
                            nc.vector.tensor_tensor(act_lo[:, at, tq:TOK], prod.unsqueeze(1),
                                                    act_hi[:, at, tq:TOK].bitcast(F32),
                                                    ALU.subtract).then_inc(prod_step, 1)
                            dve.wait_ge(prod_step, i * 2 + (l * sum(FG) + pairs + e + 1))
                    pairs += ng
                    groups += ng // 2
                    f0 += 2 * ng
                    if g == 0:
                        if l == 0:
                            with dve.Fori(0, DC // 4) as i:
                                ada_group(groups, i)
                        groups += DC // 4
                    if g:
                        for m in range(4):
                            dve.wait_ge(read_out[m], PLAN[("tile", l, f0 - 2 * ng - 4 + m)][1] + 1)
                        if g == 1:
                            with dve.Fori(0, DC // 4) as i:
                                for m in range(4):
                                    dve.wait_ge(tile_done, i * 4 + (l * TILES + f0 + m + 1))
                                    row = y[:, bass.ds(i * 4 + m, 1), tq:TOK]
                                    nc.vector.tensor_tensor(row, row, ps[m][:, 0:n_q].unsqueeze(1),
                                                            ALU.add).then_inc(read_out[m], 1)
                        else:
                            if l == 0:
                                ada_group(groups, 0)
                                add_bias(0, ADA_FIRST + ADA_MID, ADA)
                                coefficients(0, [3])
                                add_bias(1, 0, ADA)
                                coefficients(1, [0, 1, 2, 3])
                            for c in range(DC):
                                key = ("tile", l, f0 + c)
                                filled(dve, key)
                                nc.vector.tensor_tensor(y[:, c, tq:TOK], y[:, c, tq:TOK], pt(key)[:, 0:n_q],
                                                        ALU.add).then_inc(reads(key), 1)
                    f0 += DC
                add_squares(l, "post2", lambda c: dve.wait_ge(sq_ready, sq_count(l, "post2", c + 1)))
                reciprocal(l, "post2")
                residual(l, "post2", 3, y)

        @block.tensor
        def _(pe):
            uses = [0] * 4
            los = [0]

            def claim(key):
                slot, use = PLAN[key]
                if use:
                    pe.wait_ge(read_out[slot], use)
                return ps[slot]

            def pieces(a, b, t0):
                a -= t0
                b -= t0
                cuts = [a] + [512] * (a < 512 < b) + [b]
                return [(slice(p, q), slice(p + t0, q + t0)) for p, q in zip(cuts, cuts[1:])]

            def passes(dst, slot, k, tokens, width, hi, lo, kk, first, end):
                for p, (w, h) in enumerate(((w_hi, hi), (w_hi, lo), (w_lo, hi))):
                    for cols, toks in tokens:
                        mm = pe.matmul(dst[0:width, cols], w[:, slot, k, 0:width], h[:, kk, toks],
                                       start=first and p == 0, stop=end and p == 2)
                return mm

            def project(l, i, t0, width=P, ready=None):
                key = ("tile", l, i)
                n = l * TILES + i
                dst = claim(key)
                pe.wait_ge(split_done, n + 1)
                tokens = pieces(t0, TOK, t0)
                for k in range(DC):
                    if ready is not None:
                        ready(k)
                    mm = passes(dst, n % 2, k, tokens, width, h_hi, h_lo, k, k == 0, k == DC - 1)
                mm.then_inc(tile_done, 1)

            def project_values(l, ready):
                n = l * TILES + VA
                low, high = claim(("tile", l, VA)), claim(("tile", l, VD))
                pe.wait_ge(split_done, n + 2)
                for k in range(DC):
                    ready(k)
                    for b in range(NB):
                        dst = low[:, b * 256:(b + 1) * 256] if b < 4 else high[:, (b - 4) * 256:(b - 3) * 256]
                        for p, (w, h) in enumerate(((w_hi, h_hi), (w_hi, h_lo), (w_lo, h_hi))):
                            mm = pe.matmul(dst, h[:, k, b * P:(b + 1) * P], w[:, :, k, :],
                                           start=(k == 0 and p == 0 and b % 2 == 0),
                                           stop=(k == DC - 1 and p == 2), skip_group_check=True)
                mm.then_inc(tile_done, 2)

            def sums(l, name, chunks):
                key = ("sum", l, name)
                dst = claim(key)
                nh = heads_in(name)
                col = KMEAN + MEAN[name]
                for b in range(t0_of(l, name) // P, NB):
                    for n, row in enumerate(chunks):
                        mm = pe.matmul(dst[:, b * nh:(b + 1) * nh], work[:, row, b * P:(b + 1) * P],
                                       kf[:, col:col + nh], start=(n == 0), stop=(n == len(chunks) - 1))
                mm.then_inc(aux_done, 1)

            def spread(l, name):
                key = ("bc", l, name)
                dst = claim(key)
                pe.wait_ge(bcast_ready, nid(l, name) + 1)
                b0 = t0_of(l, name) // P
                for b in range(b0, NB):
                    mm = pe.matmul(dst[:, (b - b0) * P:(b - b0 + 1) * P], work[:, B_ROW, b * P:(b + 1) * P], ident,
                                   start=True, stop=True)
                mm.then_inc(aux_done, 1)

            norm_sums = [0]

            def stream_sums(l, name):
                norm_sums[0] += DC - 1
                pe.wait_ge(sum_step, norm_sums[0])
                sums(l, name, [2])
                spread(l, name)

            for l in range(LAYERS):
                last = l == LAYERS - 1
                tq = CTX if last else 0
                n_q = TOK - tq
                if l == 0:
                    pe.wait_ge(consts_in, 48)
                    pe.wait_ge(silu_done, 1)
                    dst = claim(("ada", 0))
                    for m in range(ADA_FIRST):
                        pe.wait_ge(ada_first_in[m // 2], 16)
                        for k in range(DC):
                            mm = pe.matmul(dst[:, 2 * m:2 * m + 2], ada_w[:, m, k, :], silu_t[:, k, :],
                                           start=(k == 0), stop=(k == DC - 1))
                    mm.then_inc(aux_done, 1)
                stream_sums(l, "pre1")
                lo0 = los[0]

                def h_chunk(k):
                    pe.wait_ge(lo_ready, lo0 + 2 * (k + 1))
                los[0] += 2 * DC
                project_values(l, h_chunk)
                project(l, CQ0, t0_of(l, "cq"))
                project(l, CQ1, t0_of(l, "cq"))
                project(l, CKV, 0)
                read(pe, ("tile", l, CQ1))
                sums(l, "cq", SQ["cq"])
                project(l, KR, 0, 32)
                spread(l, "cq")
                read(pe, ("tile", l, CKV))
                sums(l, "ckv", SQ["ckv"])
                project(l, QD0, tq)
                spread(l, "ckv")
                project(l, QD1, tq)
                read(pe, ("tile", l, QD0))
                sums(l, "qd0", SQ["qd0"])
                pe.wait_ge(scaled, norm_scaled(l, "cq", 2))
                pe.wait_ge(lora_in, 16 * 4 * (l + 1))
                for h in range(4):
                    dst = claim(("lq", l, h))
                    for c in range(2):
                        for cols, toks in pieces(tq, TOK, tq):
                            mm = pe.matmul(dst[0:96, cols], wuq[:, c, h * 96:(h + 1) * 96], QK[:, c, toks],
                                           start=(c == 0), stop=(c == 1))
                    mm.then_inc(aux_done, 1)
                project(l, KD, 0)
                spread(l, "qd0")
                read(pe, ("tile", l, QD1))
                sums(l, "qd1", SQ["qd1"])
                pe.wait_ge(scaled, norm_scaled(l, "ckv", 1))
                for h in range(4):
                    dst = claim(("lk", l, h))
                    for cols, toks in pieces(0, TOK, 0):
                        mm = pe.matmul(dst[0:64, cols], wukv[:, h * P:h * P + 64], QK[:, 2, toks],
                                       start=True, stop=True)
                    mm.then_inc(aux_done, 1)
                for c in range(2):
                    dst = claim(("lv", l, c))
                    for b in range(4 * c, min(4 * c + 4, NB)):
                        mm = pe.matmul(dst[:, (b - 4 * c) * 256:(b - 4 * c + 1) * 256], QK[:, 2, b * P:(b + 1) * P],
                                       wukv[:, :].rearrange("p (h e) -> p h e", e=P)[:, :, 64:P],
                                       start=True, stop=True)
                    mm.then_inc(aux_done, 1)
                project(l, QA0, tq)
                spread(l, "qd1")
                read(pe, ("tile", l, KD))
                sums(l, "kd", SQ["kd"])
                project(l, QA1, tq)
                spread(l, "kd")
                project(l, KA, 0)
                project(l, UB0, 0)
                project(l, UB1, 0)

                def maxima(h, blocks):
                    kind, _, _, _, rows, _ = HEADS[h]
                    for b in blocks:
                        key = ("max", l, h, b)
                        dst = claim(key)
                        if b == query_blocks(l)[0]:
                            pe.wait_ge(casts, 2 * (l * NH + h + 1))
                        q = cast_rows[0:rows, 0, b * P:(b + 1) * P]
                        spans = key_spans(h, b)
                        for s, (c0, k0, n, mask) in enumerate(spans):
                            mm = pe.matmul(dst[:, c0:c0 + n], q, cast_rows[0:rows, 1, k0:k0 + n],
                                           start=True, stop=not mask, skip_group_check=True)
                            for m0, side in mask:
                                mm = pe.matmul(dst[:, m0:m0 + P], id16, upper16 if side == "before" else lower16, start=False, stop=True,
                                               skip_group_check=True)
                        mm.then_inc(aux_done, 1)

                def spread_negmax(h):
                    key = ("negm", l, h)
                    dst = claim(key)
                    pe.wait_ge(diag_ready, l * NH + h + 1)
                    for cols, toks in pieces(tq, TOK, tq):
                        mm = pe.matmul(dst[:, cols], ones16, negm_diag[:, toks], start=True, stop=True)
                    mm.then_inc(aux_done, 1)

                def scores(h, j):
                    kind, q, k, _, rows, _ = HEADS[h]
                    kb = KEYS[j]
                    dst = claim(("s", l, h, j))
                    if j == 0:
                        read(pe, ("negm", l, h))
                    a, b = query_range(l, h, kb)
                    masks = []
                    if kind == "A" and kb >= CB:
                        masks = [(t, m) for t, m in (((kb - 1) * P, upper16), ((kb + 1) * P, lower16))
                                 if a <= t < b and t != kb * P and t >= CTX]
                    for cols, toks in pieces(a, b, tq):
                        inside = [(t, m) for t, m in masks if toks.start <= t < toks.stop]
                        mm = pe.matmul(dst[:, cols], QK[0:rows + 1, k, kb * P:(kb + 1) * P],
                                       QK[0:rows + 1, q, toks], start=True, stop=not inside,
                                       skip_group_check=True)
                        for n, (t, m) in enumerate(inside):
                            mm = pe.matmul(dst[:, t - tq:t - tq + P], id16, m, start=False,
                                           stop=(n == len(inside) - 1), skip_group_check=True)
                    mm.then_inc(aux_done, 1)

                def values(h, j):
                    _, _, _, v, _, _ = HEADS[h]
                    kb = KEYS[j]
                    if j == 0:
                        claim(("o", l, h))
                    dst = ps[PLAN[("o", l, h)][0]]
                    read(pe, ("s", l, h, j))
                    a, b = query_range(l, h, kb)
                    lhs = V[:, kb, v, :]
                    for cols, toks in pieces(a, b, tq):
                        mm = pe.matmul(dst[:, cols], lhs, work[:, j % 2, toks], start=(j == 0),
                                       stop=(j == len(KEYS) - 1), skip_group_check=True)
                    mm.then_inc(pv_done, 1)

                pe.wait_ge(v_ones, 5 * (l + 1))
                pe.wait_ge(krope_spread, 3 * (l + 1))
                maxima(0, query_blocks(l))
                spread_negmax(0)
                blocks = query_blocks(l)
                for h in range(NH):
                    for j in range(len(KEYS)):
                        scores(h, j)
                        if j and j < len(KEYS) - 1:
                            values(h, j - 1)
                        if h + 1 < NH and 2 <= j < 5:
                            maxima(h + 1, blocks[2 * (j - 2):2 * (j - 1)])
                    if h + 1 < NH:
                        spread_negmax(h + 1)
                    values(h, len(KEYS) - 2)
                    values(h, len(KEYS) - 1)
                    if h == 0:
                        for c in range(2):
                            key = ("pool", l, c)
                            dst = claim(key)
                            pe.wait_ge(ypool_f, 2 * l + c + 1)
                            u = work[:, 3 if c == 0 else 2, :]
                            if tq:
                                runs = [(slice(0, LAT), 3 * PAD + CTX)]
                            else:
                                runs = [(slice(0, CTX), PAD), (slice(CTX, 512), 3 * PAD + CTX),
                                        (slice(512, TOK), 3 * PAD + 512)]
                            for cols, at in runs:
                                mm = pe.matmul(dst[:, cols], poolw[:, c, :], u[:, at:at + cols.stop - cols.start],
                                               start=True, stop=True)
                            mm.then_inc(aux_done, 1)

                pe.wait_ge(head_done, (l + 1) * NH)
                for m in range(N_OUT):
                    project(l, N_IN + m, tq)
                read(pe, ("tile", l, N_IN + N_OUT - 1))
                stream_sums(l, "post1")
                stream_sums(l, "pre2")

                n_s = 1 if last else 2
                los[0] += n_s * DC
                tokens = pieces(tq, TOK, tq)
                f0 = N_IN + N_OUT
                pairs = 0
                for g, ng in enumerate(FG):
                    with pe.Fori(0, ng // 2) as i:
                        for m in range(4):
                            use = PLAN[("tile", l, f0 + m)][1]
                            pe.wait_ge(read_out[m], i + use)
                            pe.wait_ge(split_done, i * 4 + (l * TILES + f0 + m + 1))
                            for k in range(DC):
                                if g == 0 and m == 0:
                                    pe.wait_ge(lo_ready, los[0] - n_s * (DC - k - 1))
                                mm = passes(ps[m], m % 2, k, tokens, P, h_hi, h_lo, k, k == 0, k == DC - 1)
                            mm.then_inc(tile_done, 1)
                    f0 += 2 * ng
                    pairs += ng
                    with pe.Fori(0, DC // 4) as i:
                        for m in range(4):
                            use = PLAN[("tile", l, f0 + m)][1]
                            pe.wait_ge(read_out[m], i + use)
                            pe.wait_ge(split_done, i * 4 + (l * TILES + f0 + m + 1))
                            for k in range(ng):
                                if m == 0:
                                    pe.wait_ge(prod_step, l * sum(FG) + pairs - (ng - k - 1))
                                mm = passes(ps[m], m % 2, k, tokens, P, act_hi, act_lo, k, k == 0, k == ng - 1)
                            mm.then_inc(tile_done, 1)
                    f0 += DC
                stream_sums(l, "post2")


def constants(np, bf16):
    k = np.zeros((P, NCONST), np.float32)
    k[:, KID:KID + P] = np.eye(P)
    k[:, KMEAN] = 1 / D
    k[:, KMEAN + 1] = 1 / 256
    k[:, KMEAN + 2] = 1 / 128
    k[0:64, KMEAN + 3] = k[64:P, KMEAN + 4] = 1 / 64
    t = np.arange(LAT)
    row, col = (t // 64).astype(np.float32), (t % 64).astype(np.float32)
    p = np.arange(P)
    rope = np.zeros((P, 4, LAT), np.float32)
    for at, half in ((RHD, 32), (RC, 16)):
        n = half // 2
        freq = (np.float32(10000.0) ** (-np.arange(n, dtype=np.float32) / np.float32(n))).astype(np.float32)
        j = p % half
        pos = np.where((j < n)[:, None], row[None, :], col[None, :])
        ang = (pos * freq[j % n][:, None]).astype(np.float32).astype(np.float64)
        rope[:, at] = np.cos(ang)
        rope[:, at + 1] = np.sin(ang) * np.where((p // half) % 2 == 0, -1.0, 1.0)[:, None]
    for c in range(2):
        for half, size in enumerate(((2, 4), (8, 16))[c]):
            rows = slice(64 * half, 64 * half + 64)
            k[rows, KINV + c] = 1 / size
            for e, (n, first) in enumerate(((CTX, 0), (CTX, CTX - PAD), (LAT, 0), (LAT, LAT - PAD))):
                pos = np.arange(first, first + PAD)
                lo, hi = np.clip(pos - size // 2, 0, n), np.clip(pos - size // 2 + size, 0, n)
                at = KEDGE + (c * 4 + e) * PAD
                k[rows, at:at + PAD] = size / (hi - lo)
    b = np.zeros((P, 4, P), np.float32)
    i, f = np.arange(P)[:, None], np.arange(P)[None, :]
    b[:, 0] = np.eye(P)
    b[:, 1] = np.where(f >= i, 0, -1e30)
    b[:, 2] = np.where(f <= i, 0, -1e30)
    b[:, 3] = 1
    return k, b.astype(bf16), rope


def layout(np, bf16, v):
    L = LAYERS

    def tiles(w):
        l, kk, n = w.shape
        w = w.reshape(l, kk // P, P, n // P, P).transpose(0, 3, 2, 1, 4)
        if kk // P < DC:
            w = np.concatenate([w, np.zeros(w.shape[:3] + (DC - kk // P, P), w.dtype)], axis=3)
        return w

    w = v["w_in"]
    cols = {VA: 384, VD: 1568, CQ0: 768, CQ1: 896, CKV: 1024, KR: 1152, QD0: 1184, QD1: 1312, KD: 1440,
            QA0: 0, QA1: 128, KA: 256, UB0: 512, UB1: 640}
    parts = [tiles(w[:, :, cols[i]:cols[i] + P]) for i in range(N_IN)]
    parts.append(tiles(v["w_out"]))
    gate, up = tiles(v["w_gu"][:, :, :FF]), tiles(v["w_gu"][:, :, FF:])
    j = 0
    for ng in FG:
        pair = np.stack([gate[:, j:j + ng], up[:, j:j + ng]], axis=2)
        parts.append(pair.reshape(L, 2 * ng, P, DC, P))
        parts.append(tiles(v["w_down"][:, j * P:(j + ng) * P]))
        j += ng
    stream = np.concatenate(parts, axis=1).reshape(L * TILES, P, DC, P)

    def columns(a):
        return a.reshape(L, -1, P).transpose(2, 0, 1)

    def twice(a):
        return columns(np.concatenate([a, a], axis=1))

    params = np.concatenate(
        [columns(v[g]) for g in ("g_pre1", "g_post1", "g_pre2", "g_post2")]
        + [columns(v["b_ada"]), columns(v["pool_scale"]), columns(v["c_gq"]), columns(v["c_gkv"]),
           twice(v["d_gq"]), twice(v["d_gk"]), np.broadcast_to(v["a_sink"][None], (P, L, 4))], axis=2)
    x_t = np.concatenate([v["ctx"][0], v["x"][0]], axis=0).T.reshape(DC, P, TOK).transpose(1, 0, 2)
    first = ADA_FIRST * P
    ada_first = tiles(v["w_ada"][:1, :, :first])[0].transpose(1, 0, 2, 3)
    ada = v["w_ada"].transpose(0, 2, 1).reshape(L * ADA, P, D)[ADA_FIRST:]
    cond = np.concatenate([v["c"], v["c_ctx"][None]], axis=0)
    k, kb, rope = constants(np, bf16)
    blocks = np.zeros((L, P, 2, P), np.float32)
    for g in range(4):
        q = 64 * (g % 2)
        blocks[:, q:q + 64, g // 2, q:q + 64] = v["pool_w"][:, g]
    out = {
        "x_t": x_t, "cond": cond, "cond_t": cond.reshape(2, DC, P).transpose(2, 1, 0),
        "ada_first": ada_first, "ada_t": ada, "stream": stream,
        "params": params, "wuq_t": v["c_wuq"].reshape(L, 2, P, 384).transpose(0, 2, 1, 3),
        "wukv_t": v["c_wukv"], "pool_w": blocks, "consts": k, "consts_b": kb, "rope_t": rope,
    }
    return {n: np.ascontiguousarray(a) for n, a in out.items()}


def kernel(**inputs):
    import ml_dtypes
    import numpy as np
    import concourse.bacc as bacc
    from concourse.bass_utils import run_bass_kernel_spmd

    v = {n: np.asarray(a) for n, a in inputs.items()}
    arrays = layout(np, ml_dtypes.bfloat16, v)
    nc = bacc.Bacc("TRN2", target_bir_lowering=False, num_devices=1, dynamic_dma_scratch_size=1024)
    args = [nc.dram_tensor(n, a.shape, mybir.dt.from_np(a.dtype), kind="ExternalInput").ap()
            for n, a in arrays.items()]
    args.append(nc.dram_tensor("out_t", (P, DC, LAT), F32, kind="ExternalOutput").ap())
    build(nc, *args)
    r = run_bass_kernel_spmd(nc, [arrays], core_ids=[0])
    out = np.asarray(r.results[0]["out_t"])
    return np.ascontiguousarray(out.transpose(2, 1, 0).reshape(1, LAT, D))
```

```python
from contextlib import ExitStack

import concourse.bass as bass
from concourse import mybir

F32 = mybir.dt.float32
F32R = mybir.dt.float32r
BF16 = mybir.dt.bfloat16
ALU = mybir.AluOpType
ACT = mybir.ActivationFunctionType
AX = mybir.AxisListType

LAYERS = 2
P = 128
D = 1024
DC = D // P
CTX, LAT = 256, 512
TOK = CTX + LAT
NB = TOK // P
CB = CTX // P
FF = 2816
FG = (8, 8, 6)
N_IN, N_OUT = 14, DC
TILES = N_IN + N_OUT + sum(2 * j + DC for j in FG)
(VA, VD, CQ0, CQ1, CKV, KR, QD0, QD1, KD, QA0, QA1, KA, UB0, UB1) = range(N_IN)
EPS = 1e-6
PAD = 8
PW = PAD + CTX + 2 * PAD + LAT + PAD
ADA = 48
ADA_FIRST = DC
ADA_MID = 3 * DC
ADA_G = 4
MID_SLOTS = 3
MID_EARLY = {9: 3, 10: 2}
MID_TILES = (3, 2, 3, 2, 3, 2, 2, 2)
LATE = ADA_FIRST + ADA_MID
NG = 4 * DC
PB_ADA = NG
PPS = PB_ADA + ADA
PGQ, PGKV, PDGQ, PDGK, PSINK = PPS + 2, PPS + 4, PPS + 5, PPS + 6, PPS + 7
NPAR = PSINK + 4
KID, KMEAN = 0, P
KINV = KMEAN + 5
KEDGE = KINV + 2
NCONST = KEDGE + 2 * 4 * PAD
RHD, RC = 0, 2

HEADS = ([("D", 8 + h, 18 + h // 2, 2 + h // 2, 64, 12 + h) for h in range(4)]
         + [("C", 4 + h, 14 + h, 4 + h, 96, 8 + h) for h in range(4)]
         + [("A", h, 12 + h // 2, h // 2, 64, h) for h in range(4)])
NH = len(HEADS)
SCALE = {"A": 64 ** -0.5, "C": 96 ** -0.5, "D": 64 ** -0.5}
KEYS = (0, 2, 3, 4, 5, 1)

AUX = ([("sum", "pre1"), ("bc", "pre1"), ("sum", "cq"), ("bc", "cq"), ("sum", "ckv"), ("bc", "ckv"),
        ("sum", "qd0")] + [("lq", h) for h in range(4)] + [("bc", "qd0"), ("sum", "qd1")]
       + [("lk", h) for h in range(4)] + [("lv", 0), ("lv", 1), ("sum", "kd"), ("bc", "qd1"), ("bc", "kd")])
AUX2 = [("sum", "post1"), ("bc", "post1"), ("sum", "pre2"), ("bc", "pre2")]
AUX3 = [("sum", "post2"), ("bc", "post2")]
NORMS = ["pre1", "cq", "ckv", "qd0", "qd1", "kd", "post1", "pre2", "post2"]


def query_blocks(l):
    return list(range(CB if l == LAYERS - 1 else 0, NB))


def query_range(l, h, kb):
    t0 = CTX if l == LAYERS - 1 else 0
    if kb < CB:
        return t0, TOK
    if HEADS[h][0] != "A":
        return CTX, TOK
    j = kb - CB
    return CTX + P * max(j - 1, 0), CTX + P * min(j + 2, LAT // P)


def key_spans(h, b):
    if b < CB:
        return [(0, 0, CTX, [])]
    if HEADS[h][0] != "A":
        return [(0, 0, 512, []), (512, 512, TOK - 512, [])]
    first, end = max(b - 1, CB), min(b + 2, NB)
    spans = [(0, 0, CTX, [])]
    for j in range(first, end, 2):
        n = min(2, end - j)
        masks = [(CTX + (jj - first) * P, "before" if jj < b else "after") for jj in range(j, j + n) if jj != b]
        spans.append((CTX + (j - first) * P, j * P, n * P, masks))
    return spans


def keys_read(h, b):
    c0, _, n, _ = key_spans(h, b)[-1]
    return c0 + n


def product_order(l):
    qb = query_blocks(l)

    def alternate(keys):
        return [((k[0], l, *k[1:]), 2 + n % 2) for n, k in enumerate(keys)]

    order = alternate(AUX)
    if l == 0:
        order.insert(1, (("ada", l), 1))
    order += [(("tile", l, i), i % 2) for i in range(N_IN)]
    order += [(("max", l, 0, b), 3) for b in qb] + [(("negm", l, 0), 3)]
    for h in range(NH):
        for j in range(len(KEYS)):
            order.append((("s", l, h, j), j % 2))
            if h + 1 < NH and 2 <= j < 5:
                order += [(("max", l, h + 1, b), 3) for b in qb[2 * (j - 2):2 * (j - 1)]]
        if h + 1 < NH:
            order.append((("negm", l, h + 1), 3))
        order.append((("o", l, h), 2))
        if h == 1:
            order += [(("pool", l, c), 3) for c in range(2)]
    order += [(("tile", l, N_IN + m), m % 2) for m in range(N_OUT)] + alternate(AUX2)
    order += [(("tile", l, N_IN + N_OUT + f), f % 4) for f in range(TILES - N_IN - N_OUT)]
    return order + alternate(AUX3)


def psum_plan():
    plan, uses, numbers = {}, [0] * 4, {}
    for l in range(LAYERS):
        for key, slot in product_order(l):
            plan[key] = (slot, uses[slot])
            uses[slot] += 1
            if key[0] not in ("tile", "o"):
                numbers[key] = len(numbers) + 1
    return plan, numbers


PLAN, AUXN = psum_plan()


def build(nc, x_t, cond, cond_t, ada_first, ada_t, stream, params, wuq_t, wukv_t, pool_w, consts, consts_b, rope_t, out_t):
    ctx = ExitStack()
    with ctx:
        def sem(name):
            return ctx.enter_context(nc.semaphore(name))

        used = [nc.sbuf_base + (-nc.sbuf_base) % 32]

        def sb(name, shape, dt=F32, at=None):
            size = 2 if dt == BF16 else 4
            for s in shape[1:]:
                size *= s
            here = used[0] if at is None else at
            if at is None:
                used[0] = here + size + (-size) % 32
            return nc.alloc_sbuf_tensor_at(name, shape, dt, offset=here)

        xT = sb("xT", [P, DC, TOK])
        h_hi = sb("h_hi", [P, DC, TOK], F32R)
        h_lo = sb("h_lo", [P, DC, TOK], F32R)
        w_raw = sb("w_raw", [P, 2, DC, P])
        w_hi = sb("w_hi", [P, 2, DC, P], F32R)
        w_lo = sb("w_lo", [P, 2, DC, P], F32R)
        work = sb("work", [P, 6, PW])
        par = sb("par", [P, LAYERS, NPAR])
        mod = sb("mod", [P, LAYERS * ADA, 2])
        coef = sb("coef", [P, LAYERS, 4, DC, 2])
        kf = sb("kf", [P, NCONST])
        kb16 = sb("kb16", [P, 4, P], BF16)
        negmax = sb("negmax", [P, NB])
        stat = sb("stat", [P, 2, 2 * NB])
        sink8 = sb("sink8", [P, LAYERS, 4])
        adacc = sb("adacc", [P, ADA_G, 2])
        silu_t = sb("silu_t", [P, DC, 2])
        eps = sb("eps", [P, 1])
        warm = sb("warm", [P, 1])
        tick = sb("tick", [P, 2])
        phase = used[0]
        QK = sb("QK", [P, 20, TOK])
        V = sb("V", [P, NB, 9, P])
        wuq_at = used[0]
        wuq = sb("wuq", [P, 2, 384])
        cast_rows = sb("cast_rows", [P, 2, TOK], BF16, at=wuq_at)
        negm_diag = sb("negm_diag", [P, TOK], BF16)
        rope_at = used[0]
        rope_tab = sb("rope_tab", [P, 4, LAT])
        windows_ab = sb("windows_ab", [P, 2, PW], at=rope_at)
        assert 2 * PW <= 4 * LAT
        early_hi = [sb(f"early_hi{i}", [P, DC, P], F32R, at=a) for i, a in enumerate((phase + 4 * 5 * TOK, rope_at))]
        early_lo = [sb(f"early_lo{i}", [P, DC, P], F32R, at=a)
                    for i, a in enumerate((phase + 4 * (5 * TOK + D), rope_at + 4 * D))]
        assert 2 * D <= 3 * TOK and 2 * D <= 4 * LAT
        wukv = sb("wukv", [P, 512])
        poolw = sb("poolw", [P, 2, P])
        assert used[0] <= nc.sbuf_usable_end, used[0]
        ada_w = sb("ada_w", [P, DC, DC, P], at=phase)
        ada_rows = sb("ada_rows", [P, ADA_FIRST, D], at=phase + 4 * DC * D)
        cond0 = sb("cond0", [P, 2, D], at=phase + 8 * DC * D)
        mid_at = phase + 4 * 4 * TOK
        ada_mid = sb("ada_mid", [P, MID_SLOTS, D], at=mid_at)
        mid_scrap = sb("mid_scrap", [P, D], at=mid_at + 4 * MID_SLOTS * D)
        cond_mid = sb("cond_mid", [P, 2, D], at=mid_at + 4 * (MID_SLOTS + 1) * D)
        assert mid_at + 4 * (MID_SLOTS + 3) * D <= phase + 4 * 12 * TOK
        used[0] = phase
        act_hi = sb("act_hi", [P, FG[0], TOK], F32R)
        act_lo = sb("act_lo", [P, FG[0], TOK], F32R)
        y = sb("y", [P, DC, TOK])
        assert used[0] <= nc.sbuf_usable_end
        ada1 = sb("ada1", [P, 2, D])
        cond1 = sb("cond1", [P, 2, D])
        assert used[0] <= nc.sbuf_usable_end, used[0]

        silu_rows = nc.dram_tensor("silu_rows", (1, 2, D), F32, kind="Internal").ap()

        ps = [ctx.enter_context(nc.psum_tensor(f"ps{i}", [P, 1024], F32)) for i in range(4)]

        ident = kf[:, KID:KID + P]
        id16, upper16, lower16, ones16 = (kb16[:, i, :] for i in range(4))
        cos_hd, sin_hd = (rope_tab[:, RHD + i, :] for i in range(2))
        cos_c, sin_c = (rope_tab[64:96, RC + i, :] for i in range(2))

        consts_in, x_in, cond_in = sem("consts_in"), [sem("x_in0"), sem("x_in1")], sem("cond_in")
        cond_t_in, cond1_in = sem("cond_t_in"), sem("cond1_in")
        lora_in = sem("lora_in")
        ada_first_in = [sem(f"ada_first_in{i}") for i in range(DC)]
        ada_mid_in = [sem(f"ada_mid_in{i}") for i in range(MID_SLOTS)]
        ada1_in = [sem("ada1_in0"), sem("ada1_in1")]
        raw_in = [sem("raw_in0"), sem("raw_in1")]
        silu_done, silu_saved = sem("silu_done"), sem("silu_saved")
        ada_used = sem("ada_used")
        coef_ready = sem("coef_ready")
        slot_free = sem("slot_free")
        hi_made, split_done = sem("hi_made"), sem("split_done")
        tile_done = sem("tile_done")
        aux_done = sem("aux_done")
        pv_done = sem("pv_done")
        read_out = [sem(f"read_out{i}") for i in range(4)]
        dve_step = sem("dve_step")
        act_step = sem("act_step")
        sq_ready, sum_step, pool_sum = sem("sq_ready"), sem("sum_step"), sem("pool_sum")
        y_scaled = sem("y_scaled")
        rstd_ready, bcast_ready = sem("rstd_ready"), sem("bcast_ready")
        scaled, hi_ready, lo_ready = sem("scaled"), sem("hi_ready"), sem("lo_ready")
        swapped, roped = sem("swapped"), sem("roped")
        lowrank_ready = sem("lowrank_ready")
        krope_ready, krope_spread = sem("krope_ready"), sem("krope_spread")
        qc_roped = sem("qc_roped")
        v_ones, last_ones = sem("v_ones"), sem("last_ones")
        pads, pooled = sem("pads"), sem("pooled")
        pool_step = sem("pool_step")
        ypool_hi, ypool_f = sem("ypool_hi"), sem("ypool_f")
        ypool_done = sem("ypool_done")
        casts, max_done, diag_ready = sem("casts"), sem("max_done"), sem("diag_ready")
        head_done = sem("head_done")
        x_new = sem("x_new")
        prod_step = sem("prod_step")
        silu_free = sem("silu_free")
        ada_copied = sem("ada_copied")
        act_hi_made = sem("act_hi_made")
        out_done = sem("out_done")

        def filled(eng, key):
            if key[0] == "tile":
                eng.wait_ge(tile_done, key[1] * TILES + key[2] + 1)
            else:
                eng.wait_ge(aux_done, AUXN[key])

        def read(eng, key):
            slot, use = PLAN[key]
            eng.wait_ge(read_out[slot], use + 1)

        def pt(key):
            return ps[PLAN[key][0]]

        def reads(key):
            return read_out[PLAN[key][0]]

        def nid(l, name):
            return l * len(NORMS) + NORMS.index(name)

        def streams(t0):
            return [(slice(CTX, TOK), 0)] + ([(slice(0, CTX), 1)] if t0 == 0 else [])

        def t0_of(l, name):
            return CTX if l == LAYERS - 1 and name in ("qd0", "qd1", "cq", "post1", "pre2", "post2") else 0

        def heads_in(name):
            return 2 if name in ("qd0", "qd1", "kd") else 1

        def scratch(c):
            return work[:, c, 0:TOK]

        RAW = {"cq": [QK[:, 0, :], QK[:, 1, :]], "ckv": [QK[:, 2, :]],
               "qd0": [QK[:, 9, :]], "qd1": [QK[:, 11, :]], "kd": [QK[:, 19, :]]}
        SQ = {"cq": [0, 1], "ckv": [2], "qd0": [0], "qd1": [1], "kd": [2]}
        MEAN = {"pre1": 0, "post1": 0, "pre2": 0, "post2": 0, "cq": 1, "ckv": 2, "qd0": 3, "qd1": 3, "kd": 3}
        B_ROW = {name: 0 if name == "kd" else 3 for name in NORMS}

        SWAP_ROW = (4, 1)

        def sq_count(l, name, n):
            return (4 * l + ("pre1", "post1", "pre2", "post2").index(name)) * DC + n

        def rope_count(l, n):
            return 2 * (6 * l + n)

        def norm_scaled(l, name, n):
            per = [("pre1", DC), ("cq", 2), ("ckv", 1), ("qd0", 1), ("qd1", 1), ("kd", 1), ("pre2", DC)]
            total = l * sum(k for _, k in per)
            for who, k in per:
                if who == name:
                    return total + n
                total += k

        COEFS = 4 * LAYERS

        EARLY = {2: 0, N_IN + 2: 1, N_IN + N_OUT + 2: 1}

        block = ctx.enter_context(nc.Block())

        @block.sync
        def _(sp):
            sp.dma_start(kf[:, :], consts).then_inc(consts_in, 16)
            sp.dma_start(kb16[:, :, :], consts_b).then_inc(consts_in, 16)
            sp.dma_start(par[:, :, :], params).then_inc(consts_in, 16)
            sp.dma_start(silu_t[:, :, :], cond_t).then_inc(cond_t_in, 16)

            def first_scale_weights(i):
                sp.dma_start(ada_w[:, i:i + 2, :, :], ada_first[:, i:i + 2]).then_inc(ada_first_in[i], 16)

            first_scale_weights(0)
            for c in range(0, DC, 4):
                sp.dma_start(xT[:, c:c + 4, :], x_t[:, c:c + 4, :]).then_inc(x_in[c // 4], 16)
            sp.dma_start(cond0[:, :, :], cond.partition_broadcast(P)).then_inc(cond_in, 16)
            for i in range(0, DC, 2):
                if i:
                    first_scale_weights(i)
                sp.dma_start(ada_rows[:, i:i + 2, :], ada_t[i:i + 2].rearrange("m p d -> p m d")
                             ).then_inc(ada_first_in[i + 1], 16)

            def lowrank_weights(l):
                sp.dma_start(wuq[:, :, :], wuq_t[l]).then_inc(lora_in, 16)
                sp.dma_start(wukv[:, :], wukv_t[l]).then_inc(lora_in, 16)
                sp.dma_start(poolw[:, :, :], pool_w[l]).then_inc(lora_in, 16)
                sp.dma_start(rope_tab[:, :, :], rope_t).then_inc(lora_in, 16)

            for l in range(LAYERS):
                base = l * TILES
                if l == 0:
                    for n in range(2):
                        sp.dma_start(w_raw[:, n, :, :], stream[n]).then_inc(raw_in[n], 16)
                    lowrank_weights(0)
                with sp.Fori(0, TILES // 2 - 1) as i:
                    for n in range(2):
                        sp.wait_ge(split_done, i * 2 + (base + n + 1))
                        sp.dma_start(w_raw[:, n, :, :], stream[i * 2 + (base + n + 2)]).then_inc(raw_in[n], 16)
                if l + 1 < LAYERS:
                    for n in range(2):
                        sp.wait_ge(split_done, base + TILES - 1 + n)
                        sp.dma_start(w_raw[:, n, :, :], stream[base + TILES + n]).then_inc(raw_in[n], 16)
                    sp.wait_ge(tile_done, base + TILES)
                    sp.wait_ge(x_new, (2 * l + 2) * DC)
                    sp.wait_ge(ada_used, 2 * (LAYERS * ADA - DC))
                    lowrank_weights(l + 1)
            for c in range(0, DC, 2):
                sp.wait_ge(x_new, (2 * LAYERS - 1) * DC + c + 2)
                sp.dma_start(out_t[:, c:c + 2, :], xT[:, c:c + 2, CTX:TOK]).then_inc(out_done, 16)
            sp.wait_ge(out_done, 16 * (DC // 2))

        @block.gpsimd
        def _(pool):
            def split_early(l, i):
                n, slot, e = l * TILES + i, i % 2, EARLY[i]
                pool.wait_ge(raw_in[slot], 16 * (n // 2 + 1))
                nc.gpsimd.tensor_scalar(early_hi[e][:, :, :], w_raw[:, slot, :, :], 0.0, 1.0,
                                        ALU.add, ALU.mult).then_inc(hi_made, 1)
                nc.gpsimd.nop().then_inc(slot_free, 1)
                pool.wait_ge(hi_made, n + 1)
                nc.gpsimd.tensor_tensor(early_lo[e][:, :, :], w_raw[:, slot, :, :],
                                        early_hi[e][:, :, :].bitcast(F32), ALU.subtract).then_inc(split_done, 1)

            def split_one(l, i):
                n = l * TILES + i
                split(n, i % 2, 16 * (n // 2 + 1), n - 1)

            def split(n, slot, round_, used_tiles):
                pool.wait_ge(raw_in[slot], round_)
                if used_tiles is not None:
                    pool.wait_ge(tile_done, used_tiles)
                    pool.wait_ge(slot_free, n - 1)
                    nc.gpsimd.tensor_tensor(tick[:, 1:2], tick[:, 0:1], tick[:, 0:1],
                                            ALU.add).then_inc(slot_free, 1)
                nc.gpsimd.tensor_scalar(w_hi[:, slot, :, :], w_raw[:, slot, :, :], 0.0, 1.0,
                                        ALU.add, ALU.mult).then_inc(hi_made, 1)
                pool.wait_ge(hi_made, n + 1)
                nc.gpsimd.tensor_tensor(w_lo[:, slot, :, :], w_raw[:, slot, :, :],
                                        w_hi[:, slot, :, :].bitcast(F32), ALU.subtract).then_inc(split_done, 1)

            def link(ins):
                steps[0] += 1
                ins.then_inc(pool_step, 1)
                pool.wait_ge(pool_step, steps[0])

            def windows(l):
                a, b = windows_ab[:, 0, :], windows_ab[:, 1, :]
                for c in range(2):
                    u = work[:, 3, :] if c == 0 else work[:, 2, :]
                    pool.wait_ge(pads, 2 * l + c + 1)
                    read(pool, ("tile", l, UB0 + c))
                    if c == 1:
                        pool.wait_ge(ypool_f, 2 * l + 1)
                    lo, hi = 0, PW
                    rows = slice(0, P)
                    prev, cur = u, a
                    for s, (left, right) in enumerate([(-1, 0), (-1, 1), (-2, 2), (-4, 4)][:2 * c + 2]):
                        lo, hi = lo - left, hi - right
                        if s == 2 * c + 1:
                            link(nc.gpsimd.tensor_copy(cur[0:64, lo:hi], prev[0:64, lo:hi]))
                            rows = slice(64, P)
                        link(nc.gpsimd.tensor_tensor(cur[rows, lo:hi], prev[rows, lo + left:hi + left],
                                                     prev[rows, lo + right:hi + right], ALU.add))
                        prev, cur = cur, (b if cur is a else a)
                    nc.gpsimd.nop().then_inc(pooled, 1)

            pool_sums = [0]

            def add_squares(l, name):
                t0 = t0_of(l, name)
                total = work[:, 2, t0:TOK]
                for c in range(1, DC - 2):
                    pool.wait_ge(sq_ready, sq_count(l, name, c + 1))
                    if c > 1:
                        pool.wait_ge(pool_sum, pool_sums[0])
                    nc.gpsimd.tensor_tensor(total, total, work[:, c % 2, t0:TOK], ALU.add).then_inc(pool_sum, 1)
                    pool_sums[0] += 1

            nc.gpsimd.memset(tick[:, :], 0.0).then_inc(slot_free, 1)
            steps = [0]
            add_squares(0, "pre1")
            for n in range(2):
                split(n, n, 16, None)
            for l in range(LAYERS):
                base = l * TILES

                def splits(first, end):
                    with pool.Fori(first // 2, end // 2) as i:
                        for n in range(2):
                            split(i * 2 + (base + n), n, i * 16 + 16 * (base // 2 + 1), i * 2 + (base + n - 1))

                if l:
                    splits(0, 2)
                    add_squares(l, "pre1")
                if l == 0:
                    pool.wait_ge(ada_used, 2 * ADA_FIRST)
                    pool.wait_ge(aux_done, AUXN[("ada", 0)])
                else:
                    pool.wait_ge(x_new, 2 * l * DC)
                    pool.wait_ge(ada_used, 2 * (LAYERS * ADA - DC))
                split_early(l, 2)
                split_one(l, 3)
                if l == 0:
                    pool.wait_ge(silu_saved, 16)
                for n, part in enumerate((V[:, :, :, 0:64], QK[64:65, 12:14, :], QK[64:65, 18, :],
                                          QK[96:97, 14:18, :])):
                    nc.gpsimd.memset(part, 1.0).then_inc(v_ones, 1)
                    pool.wait_ge(v_ones, 4 * l + n + 1)
                splits(4, N_IN + 2)
                windows(l)
                pool.wait_ge(ypool_f, 2 * l + 2)
                split_early(l, N_IN + 2)
                split_one(l, N_IN + 3)
                splits(N_IN + 4, N_IN + N_OUT + 2)
                add_squares(l, "pre2")
                pool.wait_ge(tile_done, l * TILES + N_IN + 3)
                split_early(l, N_IN + N_OUT + 2)
                split_one(l, N_IN + N_OUT + 3)
                splits(N_IN + N_OUT + 4, TILES)

        @block.scalar
        def _(act):
            steps = [0]
            sums = [0]
            squares = [0]

            def link(ins):
                steps[0] += 1
                ins.then_inc(act_step, 1)
                act.wait_ge(act_step, steps[0])

            def act_square(out, in_):
                nc.scalar.activation(out, in_, ACT.Square).then_inc(sq_ready, 1)

            def squares_of(l, name, src, ready):
                t0 = t0_of(l, name)
                added, count = (sum_step, sums) if name == "post2" else (pool_sum, pool_sums)
                for c in range(DC):
                    ready(c)
                    if c == 0:
                        if squares[0]:
                            act.wait_ge(aux_done, last_sum[0])
                        dst = work[:, 2, t0:TOK]
                    else:
                        if c > 2:
                            act.wait_ge(added, count[0] + c - 2)
                        dst = work[:, c % 2, t0:TOK]
                    act_square(dst, src[:, c, t0:TOK])
                    squares[0] += 1
                sums[0] += DC - 1 if name == "post2" else 2
                pool_sums[0] += 0 if name == "post2" else DC - 3
                last_sum[0] = AUXN[("sum", l, name)]

            last_sum = [0]
            pool_sums = [0]

            def scale_y(l, name, which, chunks):
                t0 = t0_of(l, name)
                for c in chunks:
                    for cols, s in streams(t0):
                        nc.scalar.activation(y[:, c, cols], y[:, c, cols], ACT.Copy,
                                             scale=coef[:, l, which, c, s:s + 1]).then_inc(y_scaled, 1)

            def rms(l, name, meanwhile=None):
                key = ("sum", l, name)
                nh = heads_in(name)
                b0 = t0_of(l, name) // P
                if nh == 1 and name not in ("cq", "ckv"):
                    link(nc.scalar.activation(warm[:, :], eps[:, :], ACT.Sqrt))
                filled(act, key)
                nc.scalar.activation(stat[:, 0, b0 * nh:NB * nh], pt(key)[:, b0 * nh:NB * nh], ACT.Sqrt,
                                     bias=eps[:, 0:1]).then_inc(reads(key), 1)
                act.wait_ge(rstd_ready, nid(l, name) + 1)
                if name == "kd":
                    act.wait_ge(aux_done, AUXN[("sum", l, "qd0")])
                else:
                    if nid(l, name):
                        act.wait_ge(aux_done, last_bc[0])
                    last_bc[0] = AUXN[("bc", l, name)]
                nc.scalar.activation(
                    work[:, B_ROW[name], b0 * P:TOK].rearrange("p (b c) -> p b c", c=P // nh),
                    stat[:, 1, b0 * nh:NB * nh].unsqueeze(2).broadcast_to([P, (NB - b0) * nh, P // nh]),
                    ACT.Copy).then_inc(bcast_ready, 1)

            last_bc = [0]

            def shifts(l, name, which):
                t0 = t0_of(l, name)
                norm = 2 * l + (name == "pre2")
                for c in range(DC):
                    act.wait_ge(scaled, norm_scaled(l, name, c + 1))
                    for cols, s in streams(t0):
                        nc.scalar.activation(h_hi[:, c, cols], work[:, 4 + c % 2, cols], ACT.Identity,
                                             bias=mod[:, l * ADA + which * DC + c, s:s + 1]).then_inc(hi_ready, 1)

            def raw_and_square(l, i, name, c):
                key = ("tile", l, i)
                t0 = t0_of(l, name)
                n = TOK - t0
                filled(act, key)
                nc.scalar.activation(RAW[name][c][:, t0:TOK], pt(key)[:, 0:n], ACT.Copy).then_inc(act_step, 1)
                steps[0] += 1
                nc.scalar.activation(scratch(SQ[name][c])[:, t0:TOK], pt(key)[:, 0:n],
                                     ACT.Square).then_inc(reads(key), 1)

            ropes = [0]

            def swap_halves(src, dst_even, dst_odd, off, has_ctx, ready):
                ready()
                if has_ctx:
                    for q, dst in ((0, dst_even), (64, dst_odd)):
                        nc.scalar.activation(dst[0:64, 0:CTX], src[q:q + 64, 0:CTX],
                                             ACT.Copy).then_inc(swapped, 1)
                if ropes[0] > 2:
                    act.wait_ge(roped, ropes[0] - 2)
                row = SWAP_ROW[ropes[0] // 2 % 2]
                ropes[0] += 2
                for q in range(4):
                    nc.scalar.activation(work[32 * (q ^ 1):32 * (q ^ 1) + 32, row, 0:LAT],
                                         src[32 * q:32 * q + 32, off:off + LAT], ACT.Copy).then_inc(swapped, 1)

            act.wait_ge(dve_step, 1)
            act.wait_ge(cond_t_in, 16)
            nc.scalar.activation(silu_t[:, :, :], silu_t[:, :, :], ACT.Silu).then_inc(silu_done, 1)

            for l in range(LAYERS):
                last = l == LAYERS - 1
                if l == 0:
                    def x_ready(c):
                        act.wait_ge(x_in[c // 4], 16)
                        if c == 4:
                            act.wait_ge(cond_in, 16)
                            nc.scalar.activation(cond0[:, :, :], cond0[:, :, :], ACT.Silu).then_inc(silu_done, 1)
                            act.wait_ge(silu_done, 2)
                            act.dma_start(silu_rows, cond0[0:1, :, :]).then_inc(silu_saved, 16)

                    squares_of(l, "pre1", xT, x_ready)
                else:
                    squares_of(l, "pre1", xT, lambda c: act.wait_ge(x_new, (2 * l - 1) * DC + c + 1))
                rms(l, "pre1")
                shifts(l, "pre1", 0)
                act.wait_ge(silu_saved, 16)

                for i, b0, b1 in ((VA, 0, 4), (VD, 4, NB)):
                    key = ("tile", l, i)
                    filled(act, key)
                    nc.scalar.activation(
                        V[:, b0:b1, 0:4, 64:P],
                        pt(key)[:, 0:256 * (b1 - b0)].rearrange("p (b h d) -> p b h d", h=4, d=64),
                        ACT.Copy).then_inc(reads(key), 1)
                if l:
                    act.wait_ge(aux_done, AUXN[("sum", l, "pre1")])
                raw_and_square(l, CQ0, "cq", 0)
                raw_and_square(l, CQ1, "cq", 1)
                raw_and_square(l, CKV, "ckv", 0)
                rms(l, "cq")
                key = ("tile", l, KR)
                filled(act, key)
                nc.scalar.activation(QK[64:96, 14, :], pt(key)[0:32, 0:TOK], ACT.Copy).then_inc(reads(key), 1)
                rms(l, "ckv")
                act.wait_ge(aux_done, AUXN[("sum", l, "cq")])
                raw_and_square(l, QD0, "qd0", 0)
                for h in range(3):
                    act.wait_ge(krope_ready, l + 1)
                    nc.scalar.activation(QK[64:96, 15 + h, :], QK[64:96, 14, :], ACT.Copy).then_inc(krope_spread, 1)
                raw_and_square(l, QD1, "qd1", 0)
                rms(l, "qd0")
                tq = CTX if last else 0
                for h in range(4):
                    key = ("lq", l, h)
                    filled(act, key)
                    nc.scalar.activation(QK[0:96, 4 + h, tq:TOK], pt(key)[0:96, 0:TOK - tq],
                                         ACT.Copy).then_inc(reads(key), 1)
                act.wait_ge(aux_done, AUXN[("sum", l, "ckv")])
                raw_and_square(l, KD, "kd", 0)
                swap_halves(QK[:, 9, :], QK[:, 8, :], QK[:, 9, :], CTX, False,
                            lambda: act.wait_ge(scaled, norm_scaled(l, "qd0", 1)))
                rms(l, "qd1")
                for h in range(4):
                    key = ("lk", l, h)
                    filled(act, key)
                    nc.scalar.activation(QK[0:64, 14 + h, :], pt(key)[0:64, 0:TOK],
                                         ACT.Copy).then_inc(reads(key), 1)
                for c in range(2):
                    key = ("lv", l, c)
                    filled(act, key)
                    b0, b1 = (0, 4) if c == 0 else (4, NB)
                    nc.scalar.activation(
                        V[:, b0:b1, 4:8, 64:P],
                        pt(key)[:, 0:256 * (b1 - b0)].rearrange("p (b h d) -> p b h d", h=4, d=64),
                        ACT.Copy).then_inc(reads(key), 1)
                rms(l, "kd")

                def swap_tile(i, even):
                    key = ("tile", l, i)
                    off = 0 if last and i != KA else CTX
                    if i == QA0:
                        act.wait_ge(aux_done, AUXN[("lv", l, 1)])
                    swap_halves(pt(key), QK[:, even, :], QK[:, even + 1, :], off, off == CTX,
                                lambda: filled(act, key))

                swap_tile(QA0, 0)
                swap_halves(QK[:, 11, :], QK[:, 10, :], QK[:, 11, :], CTX, False,
                            lambda: act.wait_ge(scaled, norm_scaled(l, "qd1", 1)))
                swap_halves(QK[:, 19, :], QK[:, 18, :], QK[:, 19, :], CTX, False,
                            lambda: act.wait_ge(scaled, norm_scaled(l, "kd", 1)))
                swap_tile(QA1, 2)
                swap_tile(KA, 12)
                for c in range(2):
                    key = ("tile", l, UB0 + c)
                    dst = work[:, 3 if c == 0 else 2, :]
                    filled(act, key)
                    if c == 0:
                        act.wait_ge(aux_done, AUXN[("bc", l, "kd")])
                    act.wait_ge(pads, 2 * l + c + 1)
                    if not last:
                        link(nc.scalar.activation(dst[:, PAD:PAD + CTX], pt(key)[:, 0:CTX], ACT.Copy))
                    nc.scalar.activation(dst[:, 3 * PAD + CTX:3 * PAD + TOK], pt(key)[:, CTX - tq:TOK - tq],
                                         ACT.Copy).then_inc(reads(key), 1)

                n_q = TOK - tq

                def negmax_row(h):
                    kind, q, _, _, rows, _ = HEADS[h]
                    key = ("negm", l, h)
                    filled(act, key)
                    ins = nc.scalar.activation(QK[rows:rows + 1, q, tq:TOK], pt(key)[rows:rows + 1, 0:n_q], ACT.Copy)
                    if kind == "A":
                        link(ins)
                        act.wait_ge(head_done, l * NH // 2 + 2)
                        half = slice(64 * (h % 2), 64 * (h % 2) + 64)
                        s = PSINK + h - (NH - 4)
                        ins = nc.scalar.activation(work[half, 2 + h // 2 % 2, 0:n_q], pt(key)[half, 0:n_q], ACT.Exp,
                                                   bias=par[half, l, s:s + 1], scale=SCALE[kind])
                    ins.then_inc(reads(key), 1)

                def mid_load(n):
                    if n < ADA_MID:
                        if n >= MID_SLOTS:
                            act.wait_ge(ada_used, 2 * (ADA_FIRST + n - MID_SLOTS + 1))
                        act.dma_start(ada_mid[:, n % MID_SLOTS, :], ada_t[ADA_FIRST + n]
                                      ).then_inc(ada_mid_in[n % MID_SLOTS], 16)

                negmax_row(0)
                loaded = MID_SLOTS
                for h in range(NH):
                    kind = HEADS[h][0]
                    for j, kb in enumerate(KEYS):
                        u = (l * NH + h) * len(KEYS) + j
                        key = ("s", l, h, j)
                        a, b = query_range(l, h, kb)
                        filled(act, key)
                        if u >= 2:
                            act.wait_ge(pv_done, u - 1)
                        nc.scalar.activation(work[:, j % 2, a:b], pt(key)[:, a - tq:b - tq], ACT.Exp,
                                             scale=SCALE[kind]).then_inc(reads(key), 1)
                    if h + 1 < NH:
                        negmax_row(h + 1)
                    if l == 0 and h == NH - 4:
                        act.dma_start(cond_mid[:, :, :], silu_rows[0].partition_broadcast(P)).then_inc(cond_in, 16)
                        for n in range(MID_SLOTS):
                            mid_load(n)
                    if l == 0 and h - 1 in MID_EARLY:
                        for n in range(MID_EARLY[h - 1]):
                            mid_load(loaded)
                            loaded += 1
                    act.wait_ge(pv_done, (l * NH + h + 1) * len(KEYS))
                    if h and h % 2 == 0:
                        act.wait_ge(head_done, (l * NH + h) // 2)
                    half = slice(64 * (h % 2), 64 * (h % 2) + 64)
                    other = slice(64 - 64 * (h % 2), P - 64 * (h % 2))
                    o = pt(("o", l, h))
                    link(nc.scalar.activation(work[half, 4, 0:n_q], o[half, 0:n_q], ACT.Copy))
                    nc.scalar.activation(work[half, 5, 0:n_q], o[other, 0:n_q], ACT.Copy).then_inc(read_out[2], 1)

                t0 = tq
                act.wait_ge(head_done, (l + 1) * NH // 2)
                if l == 0:
                    act.dma_start(cond1[:, :, :], silu_rows[0].partition_broadcast(P)).then_inc(cond1_in, 16)
                    for m in range(2):
                        act.dma_start(ada1[:, m, :], ada_t[LATE + m]).then_inc(ada1_in[m], 16)
                for c in range(DC):
                    key = ("tile", l, N_IN + c)
                    if l == 0 and c:
                        for n in range(MID_TILES[c - 1]):
                            mid_load(loaded)
                            loaded += 1
                    filled(act, key)
                    if c > 2:
                        act.wait_ge(sum_step, sums[0] + c - 2)
                    dst = work[:, 2, t0:TOK] if c == 0 else work[:, c % 2, t0:TOK]
                    nc.scalar.activation(dst, pt(key)[:, 0:n_q], ACT.Square).then_inc(sq_ready, 1)
                    nc.scalar.activation(y[:, c, t0:TOK], pt(key)[:, 0:n_q], ACT.Copy).then_inc(reads(key), 1)
                sums[0] += DC - 1
                last_sum[0] = AUXN[("sum", l, "post1")]
                read(act, key)
                rms(l, "post1")
                act.wait_ge(coef_ready, 3 if l == 0 else COEFS)
                scale_y(l, "post1", 1, range(DC))
                squares_of(l, "pre2", xT, lambda c: act.wait_ge(x_new, 2 * l * DC + c + 1))
                rms(l, "pre2")
                shifts(l, "pre2", 3)
                def ada_load(first, i, m):
                    act.wait_ge(ada_used, i * (2 * ADA_G) + 2 * (LATE + ADA_G * first + m + 1))
                    act.dma_start(ada1[:, m % 2, :], ada_t[i * ADA_G + (LATE + ADA_G * first + m + 2)]
                                  ).then_inc(ada1_in[m % 2], 16)

                pairs = 0
                groups = 0
                f0 = N_IN + N_OUT
                for g, ng in enumerate(FG):
                    with act.Fori(0, ng // 2) as i:
                        for e in range(2):
                            if l == 0:
                                for m in (2 * e, 2 * e + 1):
                                    ada_load(groups, i, m)
                            act.wait_ge(tile_done, i * 4 + (l * TILES + f0 + 2 * e + 1))
                            act.wait_ge(silu_free, i * 2 + (l * sum(FG) + pairs + e + 1))
                            nc.scalar.activation(work[:, e, t0:TOK], ps[2 * e][:, 0:n_q],
                                                 ACT.Silu).then_inc(read_out[2 * e], 1)
                    pairs += ng
                    groups += ng // 2
                    f0 += 2 * ng
                    if g == 0:
                        with act.Fori(0, DC // 4) as i:
                            for m in range(4):
                                if l == 0:
                                    ada_load(groups, i, m)
                                act.wait_ge(tile_done, i * 4 + (l * TILES + f0 + m + 1))
                                nc.scalar.activation(y[:, bass.ds(i * 4 + m, 1), t0:TOK],
                                                     ps[m][:, 0:n_q].unsqueeze(1), ACT.Copy).then_inc(read_out[m], 1)
                        groups += DC // 4
                    if l == 0 and g == len(FG) - 1:
                        for m in range(2):
                            ada_load(groups, 0, m)
                    f0 += DC
                squares_of(l, "post2", y, lambda c: read(act, ("tile", l, TILES - DC + c)))
                act.wait_ge(sq_ready, sq_count(l, "post2", DC))
                rms(l, "post2")
                act.wait_ge(coef_ready, COEFS)
                scale_y(l, "post2", 3, range(DC))

        @block.vector
        def _(dve):
            steps = [0]
            sums = [0]
            his = [0]
            swaps = [0]
            los = [0]
            xs = [0]
            mids = [0]
            ropes = [0]
            ys = [0]

            def link(ins):
                steps[0] += 1
                ins.then_inc(dve_step, 1)
                dve.wait_ge(dve_step, steps[0])

            def add_squares(l, name, ready):
                t0 = t0_of(l, name)
                total = work[:, 2, t0:TOK]
                for c in range(1, DC):
                    ready(c)
                    if c > 1:
                        dve.wait_ge(sum_step, sums[0])
                    nc.vector.tensor_tensor(total, total, work[:, c % 2, t0:TOK], ALU.add).then_inc(sum_step, 1)
                    sums[0] += 1

            def add_last_squares(l, name):
                t0 = t0_of(l, name)
                total = work[:, 2, t0:TOK]
                pool_sums[0] += DC - 3
                dve.wait_ge(pool_sum, pool_sums[0])
                for c in (DC - 2, DC - 1):
                    dve.wait_ge(sq_ready, sq_count(l, name, c + 1))
                    nc.vector.tensor_tensor(total, total, work[:, c % 2, t0:TOK], ALU.add).then_inc(sum_step, 1)
                    sums[0] += 1
                    dve.wait_ge(sum_step, sums[0])

            pool_sums = [0]

            def reciprocal(l, name):
                nh = heads_in(name)
                b0 = t0_of(l, name) // P
                read(dve, ("sum", l, name))
                nc.vector.reciprocal(stat[:, 1, b0 * nh:NB * nh],
                                     stat[:, 0, b0 * nh:NB * nh]).then_inc(rstd_ready, 1)

            def modulate(l, name, which):
                t0 = t0_of(l, name)
                key = ("bc", l, name)
                filled(dve, key)
                n_s = len(streams(t0))

                def low(c):
                    dve.wait_ge(hi_ready, his[0] + n_s)
                    his[0] += n_s
                    for cols, s in streams(t0):
                        nc.vector.scalar_tensor_tensor(
                            out=h_lo[:, c, cols], in0=work[:, 4 + c % 2, cols],
                            scalar=mod[:, l * ADA + which * DC + c, s:s + 1], in1=h_hi[:, c, cols].bitcast(F32),
                            op0=ALU.add, op1=ALU.subtract).then_inc(lo_ready, 1)
                        los[0] += 1

                for c in range(DC):
                    if c >= 2:
                        low(c - 2)
                        dve.wait_ge(lo_ready, los[0])
                    for n, (cols, s) in enumerate(streams(t0)):
                        ins = nc.vector.scalar_tensor_tensor(
                            out=work[:, 4 + c % 2, cols], in0=xT[:, c, cols],
                            scalar=coef[:, l, 0 if name == "pre1" else 2, c, s:s + 1],
                            in1=pt(key)[:, cols.start - t0:cols.stop - t0], op0=ALU.mult, op1=ALU.mult)
                        if n + 1 < n_s:
                            ins.then_inc(dve_step, 1)
                            steps[0] += 1
                    ins.then_inc(scaled, 1)
                low(DC - 2)
                low(DC - 1)
                dve.wait_ge(lo_ready, los[0])

            def residual(l, name):
                t0 = t0_of(l, name)
                key = ("bc", l, name)
                filled(dve, key)

                def product(c):
                    ys[0] += len(streams(t0))
                    dve.wait_ge(y_scaled, ys[0])
                    if c >= 2:
                        dve.wait_ge(x_new, xs[0])
                    nc.vector.tensor_tensor(work[:, 4 + c % 2, t0:TOK], y[:, c, t0:TOK],
                                            pt(key)[:, 0:TOK - t0], ALU.mult).then_inc(dve_step, 1)
                    steps[0] += 1

                product(0)
                for c in range(DC):
                    made = steps[0]
                    if c + 1 < DC:
                        product(c + 1)
                    dve.wait_ge(dve_step, made)
                    nc.vector.tensor_tensor(xT[:, c, t0:TOK], xT[:, c, t0:TOK], work[:, 4 + c % 2, t0:TOK],
                                            ALU.add).then_inc(x_new, 1)
                    xs[0] += 1
                dve.wait_ge(x_new, xs[0])
                release(key)

            def release(key):
                dve.wait_ge(dve_step, steps[0])
                dve.nop().then_inc(reads(key), 1)

            def apply_norm(l, name, gain):
                t0 = t0_of(l, name)
                key = ("bc", l, name)
                filled(dve, key)
                for c, raw in enumerate(RAW[name]):
                    nc.vector.scalar_tensor_tensor(
                        out=raw[:, t0:TOK], in0=raw[:, t0:TOK], scalar=par[:, l, gain + c:gain + c + 1],
                        in1=pt(key)[:, 0:TOK - t0], op0=ALU.mult, op1=ALU.mult).then_inc(scaled, 1)
                dve.wait_ge(scaled, norm_scaled(l, name, len(RAW[name])))
                dve.nop().then_inc(reads(key), 1)

            def rope(src, dst_even, dst_odd, off, has_ctx, key=None):
                swaps[0] += 4 + 2 * has_ctx
                dve.wait_ge(swapped, swaps[0])
                row = SWAP_ROW[ropes[0] % 2]
                ropes[0] += 1
                t1, t2 = work[:, 5, 0:LAT], work[:, row, 0:LAT]
                ins = nc.vector.tensor_tensor(t1, src[:, off:off + LAT], cos_hd, ALU.mult)
                link(ins)
                if key is not None:
                    dve.nop().then_inc(reads(key), 1)
                link(nc.vector.tensor_tensor(t2, t2, sin_hd, ALU.mult))
                if key is None:
                    for q, dst in ((0, dst_even), (64, dst_odd)):
                        if src_ctx[0]:
                            link(nc.vector.tensor_copy(dst[0:64, 0:CTX], src[q:q + 64, 0:CTX]))
                for q, dst in ((0, dst_even), (64, dst_odd)):
                    nc.vector.tensor_tensor(dst[0:64, CTX:TOK], work[q:q + 64, 5, 0:LAT],
                                            work[q:q + 64, row, 0:LAT], ALU.add).then_inc(roped, 1)

            src_ctx = [True]

            def rope_c(tile):
                x = QK[64:96, tile, CTX:TOK]
                t1, t2 = work[64:96, 5, 0:LAT], work[64:96, 4, 0:LAT]
                link(nc.vector.stream_shuffle(t2, x, list(range(16, 32)) + list(range(16))))
                link(nc.vector.tensor_tensor(t1, x, cos_c, ALU.mult))
                link(nc.vector.tensor_tensor(t2, t2, sin_c, ALU.mult))
                return nc.vector.tensor_tensor(x, t1, t2, ALU.add)

            def add_bias(l, first, end, values=None):
                m = mod[:, l * ADA + first:l * ADA + end, :]
                b = par[:, l, PB_ADA + first:PB_ADA + end].unsqueeze(2).broadcast_to([P, end - first, 2])
                link(nc.vector.tensor_tensor(m, m if values is None else values, b, ALU.add))

            coefs = [0]

            def coefficients(l, norms):
                for n in norms:
                    vec, plus = ((1, 1.0), (2, 0.0), (4, 1.0), (5, 0.0))[n]
                    g = par[:, l, n * DC:(n + 1) * DC].unsqueeze(2).broadcast_to([P, DC, 2])
                    at = l * ADA + vec * DC
                    nc.vector.scalar_tensor_tensor(out=coef[:, l, n, :, :], in0=mod[:, at:at + DC, :],
                                                   scalar=plus, in1=g, op0=ALU.add, op1=ALU.mult
                                                   ).then_inc(coef_ready, 1)
                    coefs[0] += 1
                dve.wait_ge(coef_ready, coefs[0])

            scrap = work[:, 4:6, :].rearrange("p a b -> p (a b)")[:, 0:D]

            def dot(weights, cond, s, out, after, scrap):
                if after is not None:
                    dve.wait_ge(ada_used, after)
                nc.vector.tensor_tensor_reduce(weights if s else scrap, weights, cond[:, s, :], 1.0, 0.0,
                                               ALU.mult, ALU.add, out).then_inc(ada_used, 1)

            link(nc.vector.memset(eps[:, :], EPS))
            dve.nop().then_inc(silu_free, 1)
            dve.nop().then_inc(silu_free, 1)
            dve.wait_ge(consts_in, 48)
            link(nc.vector.tensor_scalar(sink8[:, :, :], par[:, :, PSINK:PSINK + 4], -1.0 / SCALE["A"], None, ALU.mult))

            dve.wait_ge(silu_done, 2)
            for n in range(ADA_FIRST):
                if n == 3:
                    add_last_squares(0, "pre1")
                if n % 2 == 0:
                    dve.wait_ge(ada_first_in[n + 1], 16)
                for s in range(2):
                    dot(ada_rows[:, n, :], cond0, s, mod[:, n, s:s + 1], 2 * n + s or None, scrap)
                if n == ADA_FIRST - 3:
                    reciprocal(0, "pre1")
            dve.wait_ge(ada_used, 2 * ADA_FIRST)
            add_bias(0, 0, ADA_FIRST)

            for l in range(LAYERS):
                last = l == LAYERS - 1
                tq = CTX if last else 0
                n_q = TOK - tq
                if l:
                    add_last_squares(l, "pre1")
                    reciprocal(l, "pre1")
                if l == 0:
                    key = ("ada", 0)
                    filled(dve, key)
                    add_bias(0, DC, 2 * DC, pt(key)[:, 0:2 * DC].rearrange("p (m s) -> p m s", s=2))
                    dve.nop().then_inc(reads(key), 1)
                    coefficients(0, [0])
                modulate(l, "pre1", 0)
                release(("bc", l, "pre1"))
                dve.wait_ge(lora_in, 16 * 4 * (l + 1))
                reciprocal(l, "cq")
                reciprocal(l, "ckv")
                apply_norm(l, "cq", PGQ)
                read(dve, ("tile", l, KR))
                rope_c(14).then_inc(krope_ready, 1)
                apply_norm(l, "ckv", PGKV)
                reciprocal(l, "qd0")
                for h in range(4):
                    read(dve, ("lq", l, h))
                    if h == 0:
                        dve.wait_ge(krope_ready, l + 1)
                    else:
                        dve.wait_ge(qc_roped, 4 * l + h)
                    rope_c(4 + h).then_inc(qc_roped, 1)
                dve.wait_ge(qc_roped, 4 * l + 4)
                apply_norm(l, "qd0", PDGQ)
                src_ctx[0] = not last
                rope(QK[:, 9, :], QK[:, 8, :], QK[:, 9, :], CTX, False)
                reciprocal(l, "qd1")
                reciprocal(l, "kd")

                cast_q, cast_k = cast_rows[:, 0, :], cast_rows[:, 1, :]

                def cast(h):
                    _, q, k, _, rows, _ = HEADS[h]
                    if h:
                        dve.wait_ge(aux_done, AUXN[("max", l, h - 1, NB - 1)])
                    nc.vector.tensor_copy(cast_q[0:rows, tq:TOK], QK[0:rows, q, tq:TOK]).then_inc(casts, 1)
                    nc.vector.tensor_copy(cast_k[0:rows, :], QK[0:rows, k, :]).then_inc(casts, 1)

                def rope_tile(n, i, even):
                    key = ("tile", l, i)
                    off = 0 if last and i != KA else CTX
                    dve.wait_ge(roped, rope_count(l, n))
                    rope(pt(key), QK[:, even, :], QK[:, even + 1, :], off, off == CTX, key)

                apply_norm(l, "qd1", PDGQ)
                apply_norm(l, "kd", PDGK)
                rope_tile(1, QA0, 0)
                dve.wait_ge(roped, rope_count(l, 2))
                rope(QK[:, 11, :], QK[:, 10, :], QK[:, 11, :], CTX, False)
                src_ctx[0] = True
                dve.wait_ge(roped, rope_count(l, 3))
                rope(QK[:, 19, :], QK[:, 18, :], QK[:, 19, :], CTX, False)
                dve.wait_ge(roped, rope_count(l, 4))
                read(dve, ("lk", l, 3))
                dve.wait_ge(krope_spread, 3 * (l + 1))
                cast(0)
                rope_tile(4, QA1, 2)
                rope_tile(5, KA, 12)
                dve.wait_ge(roped, rope_count(l, 6))
                nc.vector.memset(QK[64:65, 19, :], 1.0).then_inc(last_ones, 1)
                for c in range(2):
                    u = work[:, 3 if c == 0 else 2, :]
                    dve.wait_ge(aux_done, AUXN[("bc", l, "kd")])
                    link(nc.vector.memset(u[:, 0:PAD], 0.0))
                    link(nc.vector.memset(u[:, PAD + CTX:3 * PAD + CTX], 0.0))
                    nc.vector.memset(u[:, PW - PAD:PW], 0.0).then_inc(pads, 1)

                def mid_dots(chunks):
                    for n in range(mids[0], mids[0] + chunks):
                        dve.wait_ge(ada_mid_in[n % MID_SLOTS], 16 * (n // MID_SLOTS + 1))
                        for s in range(2):
                            dot(ada_mid[:, n % MID_SLOTS, :], cond_mid, s, mod[:, 2 * DC + n, s:s + 1],
                                2 * (ADA_FIRST + n) + s, mid_scrap[:, :])
                    mids[0] += chunks

                def maxima(h, between=()):
                    kind = HEADS[h][0]
                    between = iter(between)
                    if l or h:
                        dve.wait_ge(diag_ready, l * NH + h)
                    for b in query_blocks(l):
                        key = ("max", l, h, b)
                        filled(dve, key)
                        nc.vector.tensor_reduce(negmax[:, b:b + 1], pt(key)[:, 0:keys_read(h, b)], AX.X, ALU.max,
                                                negate=True).then_inc(reads(key), 1)
                        next(between, None)
                    for _ in between:
                        pass
                    read(dve, key)
                    b0 = tq // P
                    if kind == "A":
                        s = h - (NH - 4)
                        link(nc.vector.tensor_scalar(negmax[:, b0:NB], negmax[:, b0:NB], sink8[:, l, s:s + 1], None,
                                                     ALU.min))
                    if h:
                        filled(dve, ("negm", l, h - 1))
                    nc.vector.tensor_tensor(
                        negm_diag[:, tq:TOK].rearrange("p (b c) -> p b c", c=P),
                        id16.unsqueeze(1).broadcast_to([P, NB - b0, P]),
                        negmax[:, b0:NB].unsqueeze(2).broadcast_to([P, NB - b0, P]), ALU.mult).then_inc(diag_ready, 1)

                def finish(h):
                    kind, _, _, _, _, chunk = HEADS[h]
                    read(dve, ("o", l, h))
                    o, den = work[:, 4, 0:n_q], work[:, 5, 0:n_q]
                    if kind == "A":
                        link(nc.vector.tensor_tensor(den, den, work[:, 2 + h // 2 % 2, 0:n_q], ALU.add))
                    link(nc.vector.reciprocal(den, den))
                    yield
                    link(nc.vector.tensor_tensor(o, o, den, ALU.mult))
                    yield
                    hi = h_hi[:, chunk // 2, tq:TOK]
                    link(nc.vector.tensor_copy(hi, o))
                    yield
                    nc.vector.tensor_tensor(h_lo[:, chunk // 2, tq:TOK], o, hi.bitcast(F32),
                                            ALU.subtract).then_inc(head_done, 1)
                    dve.wait_ge(head_done, (l * NH + h + 1) // 2)

                maxima(0)
                cast(1)
                for h in range(NH):
                    pair = finish(h - 1) if h and h % 2 == 0 else iter(())
                    next(pair, None)
                    if h + 1 < NH:
                        maxima(h + 1, pair)
                    if h + 2 < NH:
                        cast(h + 2)
                    if l == 0 and h in MID_EARLY:
                        if not mids[0]:
                            dve.wait_ge(cond_in, 32)
                        mid_dots(MID_EARLY[h])
                    if h < 2:
                        for c in (h,):
                            u = work[:, 3 if c == 0 else 2, :]
                            dve.wait_ge(pooled, 2 * l + c + 1)
                            s = windows_ab[:, 1, :]
                            for e, at in enumerate((PAD, CTX, 3 * PAD + CTX, 2 * PAD + TOK)):
                                k = KEDGE + (c * 4 + e) * PAD
                                link(nc.vector.tensor_tensor(s[:, at:at + PAD], s[:, at:at + PAD], kf[:, k:k + PAD], ALU.mult))
                            ins = nc.vector.scalar_tensor_tensor(
                                out=u[:, PAD:PW - PAD], in0=s[:, PAD:PW - PAD], scalar=kf[:, KINV + c:KINV + c + 1],
                                in1=u[:, PAD:PW - PAD], op0=ALU.mult, op1=ALU.subtract)
                            ins.then_inc(ypool_f, 1)
                    if h == 1:
                        for c in range(2):
                            key = ("pool", l, c)
                            filled(dve, key)
                            f = work[:, 3, 0:n_q]
                            link(nc.vector.tensor_scalar(f, pt(key)[:, 0:n_q], par[:, l, PPS + c:PPS + c + 1], None,
                                                         ALU.mult))
                            dve.nop().then_inc(reads(key), 1)
                            link(nc.vector.tensor_copy(h_hi[:, 2 + c, tq:TOK], f))
                            link(nc.vector.tensor_tensor(h_lo[:, 2 + c, tq:TOK], f,
                                                         h_hi[:, 2 + c, tq:TOK].bitcast(F32), ALU.subtract))
                for _ in finish(NH - 1):
                    pass

                def square_ready(c):
                    if l == 0:
                        if c == 1:
                            mid_dots(MID_TILES[0])
                        mid_dots(MID_TILES[c])
                    dve.wait_ge(sq_ready, sq_count(l, "post1", c + 1))

                add_squares(l, "post1", square_ready)
                if l == 0:
                    dve.wait_ge(ada_used, 2 * LATE)
                    add_bias(0, 2 * DC, 2 * DC + ADA_MID)
                    coefficients(0, [1, 2])
                reciprocal(l, "post1")
                residual(l, "post1")
                add_last_squares(l, "pre2")
                reciprocal(l, "pre2")
                modulate(l, "pre2", 3)
                release(("bc", l, "pre2"))

                pairs = 0
                f0 = N_IN + N_OUT
                groups = 0

                def ada_group(first, i):
                    if first == 0:
                        dve.wait_ge(cond1_in, 16)
                    for m in range(ADA_G):
                        dve.wait_ge(ada1_in[m % 2], i * 32 + (32 * first + 16 * (m // 2) + 16))
                        for s in range(2):
                            dot(ada1[:, m % 2, :], cond1, s, adacc[:, m, s:s + 1],
                                i * (2 * ADA_G) + (2 * (LATE + ADA_G * first + m) + s), scrap)
                    dve.wait_ge(ada_used, i * (2 * ADA_G) + 2 * (LATE + ADA_G * (first + 1)))
                    dst = mod[:, bass.ds(i * ADA_G + (DC + LATE + first * ADA_G), ADA_G), :]
                    nc.vector.tensor_copy(dst, adacc[:, :, :]).then_inc(ada_copied, 1)
                    dve.wait_ge(ada_copied, i + (first + 1))

                for g, ng in enumerate(FG):
                    with dve.Fori(0, ng // 2) as i:
                        if l == 0:
                            ada_group(groups, i)
                        for e in range(2):
                            dve.wait_ge(tile_done, i * 4 + (l * TILES + f0 + 2 * e + 2))
                            dve.wait_ge(read_out[2 * e], i + (PLAN[("tile", l, f0 + 2 * e)][1] + 1))
                            prod = work[:, 2 + e, tq:TOK]
                            nc.vector.tensor_tensor(prod, work[:, e, tq:TOK], ps[2 * e + 1][:, 0:n_q],
                                                    ALU.mult).then_inc(read_out[2 * e + 1], 1)
                            dve.wait_ge(read_out[2 * e + 1], i + (PLAN[("tile", l, f0 + 2 * e + 1)][1] + 1))
                            at = bass.ds(i * 2 + e, 1)
                            nc.vector.tensor_copy(act_hi[:, at, tq:TOK], prod.unsqueeze(1)).then_inc(act_hi_made, 1)
                            dve.nop().then_inc(silu_free, 1)
                            dve.wait_ge(act_hi_made, i * 2 + (l * sum(FG) + pairs + e + 1))
                            nc.vector.tensor_tensor(act_lo[:, at, tq:TOK], prod.unsqueeze(1),
                                                    act_hi[:, at, tq:TOK].bitcast(F32),
                                                    ALU.subtract).then_inc(prod_step, 1)
                            dve.wait_ge(prod_step, i * 2 + (l * sum(FG) + pairs + e + 1))
                    pairs += ng
                    groups += ng // 2
                    f0 += 2 * ng
                    if g == 0:
                        if l == 0:
                            with dve.Fori(0, DC // 4) as i:
                                ada_group(groups, i)
                        groups += DC // 4
                    if g:
                        for m in range(4):
                            dve.wait_ge(read_out[m], PLAN[("tile", l, f0 - 2 * ng - 4 + m)][1] + 1)
                        if g == 1:
                            with dve.Fori(0, DC // 4) as i:
                                for m in range(4):
                                    dve.wait_ge(tile_done, i * 4 + (l * TILES + f0 + m + 1))
                                    row = y[:, bass.ds(i * 4 + m, 1), tq:TOK]
                                    nc.vector.tensor_tensor(row, row, ps[m][:, 0:n_q].unsqueeze(1),
                                                            ALU.add).then_inc(read_out[m], 1)
                        else:
                            if l == 0:
                                ada_group(groups, 0)
                                add_bias(0, DC + LATE, ADA)
                                coefficients(0, [3])
                                add_bias(1, 0, ADA)
                                coefficients(1, [0, 1, 2, 3])

                            def add_tile(c):
                                key = ("tile", l, f0 + c)
                                filled(dve, key)
                                nc.vector.tensor_tensor(y[:, c, tq:TOK], y[:, c, tq:TOK], pt(key)[:, 0:n_q],
                                                        ALU.add).then_inc(reads(key), 1)

                            def next_square(c):
                                if c + 1 < DC:
                                    add_tile(c + 1)
                                dve.wait_ge(sq_ready, sq_count(l, "post2", c + 1))

                            add_tile(0)
                            add_tile(1)
                            add_squares(l, "post2", next_square)
                    f0 += DC
                reciprocal(l, "post2")
                residual(l, "post2")

        @block.tensor
        def _(pe):
            uses = [0] * 4
            los = [0]

            def claim(key):
                slot, use = PLAN[key]
                if use:
                    pe.wait_ge(read_out[slot], use)
                return ps[slot]

            def pieces(a, b, t0):
                a -= t0
                b -= t0
                cuts = [a] + [512] * (a < 512 < b) + [b]
                return [(slice(p, q), slice(p + t0, q + t0)) for p, q in zip(cuts, cuts[1:])]

            def passes(dst, slot, k, tokens, width, hi, lo, kk, first, end, early=None):
                whi, wlo = w_hi[:, slot, k, 0:width], w_lo[:, slot, k, 0:width]
                if early is not None:
                    whi, wlo = early_hi[early][:, k, 0:width], early_lo[early][:, k, 0:width]
                for p, (w, h) in enumerate(((whi, hi), (whi, lo), (wlo, hi))):
                    for cols, toks in tokens:
                        mm = pe.matmul(dst[0:width, cols], w, h[:, kk, toks],
                                       start=first and p == 0, stop=end and p == 2)
                return mm

            def project(l, i, t0, width=P, ready=None):
                key = ("tile", l, i)
                n = l * TILES + i
                dst = claim(key)
                pe.wait_ge(split_done, n + 1)
                tokens = pieces(t0, TOK, t0)
                for k in range(DC):
                    if ready is not None:
                        ready(k)
                    mm = passes(dst, n % 2, k, tokens, width, h_hi, h_lo, k, k == 0, k == DC - 1, EARLY.get(i))
                mm.then_inc(tile_done, 1)

            def project_values(l, ready):
                n = l * TILES + VA
                low, high = claim(("tile", l, VA)), claim(("tile", l, VD))
                pe.wait_ge(split_done, n + 2)
                for k in range(DC):
                    ready(k)
                    for b in range(NB):
                        dst = low[:, b * 256:(b + 1) * 256] if b < 4 else high[:, (b - 4) * 256:(b - 3) * 256]
                        for p, (w, h) in enumerate(((w_hi, h_hi), (w_hi, h_lo), (w_lo, h_hi))):
                            mm = pe.matmul(dst, h[:, k, b * P:(b + 1) * P], w[:, :, k, :],
                                           start=(k == 0 and p == 0 and b % 2 == 0),
                                           stop=(k == DC - 1 and p == 2), skip_group_check=True)
                mm.then_inc(tile_done, 2)

            def sums(l, name, chunks, ready=None):
                key = ("sum", l, name)
                dst = claim(key)
                nh = heads_in(name)
                col = KMEAN + MEAN[name]
                b0 = t0_of(l, name) // P
                for n, row in enumerate(chunks):
                    if ready is not None:
                        ready(n)
                    for b in range(b0, NB):
                        mm = pe.matmul(dst[:, b * nh:(b + 1) * nh], work[:, row, b * P:(b + 1) * P],
                                       kf[:, col:col + nh], start=(n == 0 and b == b0),
                                       stop=(n == len(chunks) - 1), skip_group_check=True)
                mm.then_inc(aux_done, 1)

            def spread(l, name):
                key = ("bc", l, name)
                dst = claim(key)
                pe.wait_ge(bcast_ready, nid(l, name) + 1)
                b0 = t0_of(l, name) // P
                for b in range(b0, NB):
                    mm = pe.matmul(dst[:, (b - b0) * P:(b - b0 + 1) * P], work[:, B_ROW[name], b * P:(b + 1) * P], ident,
                                   start=True, stop=True)
                mm.then_inc(aux_done, 1)

            norm_sums = [0]

            def first_scale(first, end):
                pe.wait_ge(silu_done, 1)
                dst = claim(("ada", 0))
                for m in range(first, end):
                    if m % 2 == 0:
                        pe.wait_ge(ada_first_in[m], 16)
                    for k in range(DC):
                        mm = pe.matmul(dst[:, 2 * m:2 * m + 2], ada_w[:, m, k, :], silu_t[:, k, :],
                                       start=(k == 0), stop=(k == DC - 1))
                if end == DC:
                    mm.then_inc(aux_done, 1)

            def stream_sums(l, name):
                norm_sums[0] += 2 if name in ("pre1", "pre2") else DC - 1
                pe.wait_ge(sum_step, norm_sums[0])
                sums(l, name, [2])
                if (l, name) == (0, "pre1"):
                    first_scale(DC // 2, DC)
                spread(l, name)

            for l in range(LAYERS):
                last = l == LAYERS - 1
                tq = CTX if last else 0
                n_q = TOK - tq
                if l == 0:
                    pe.wait_ge(consts_in, 48)
                    first_scale(0, DC // 2)
                stream_sums(l, "pre1")
                lo0 = los[0]

                def h_chunk(k):
                    pe.wait_ge(lo_ready, lo0 + 2 * (k + 1))
                los[0] += 2 * DC
                project_values(l, h_chunk)
                project(l, CQ0, t0_of(l, "cq"))
                project(l, CQ1, t0_of(l, "cq"))
                project(l, CKV, 0)
                read(pe, ("tile", l, CQ1))
                sums(l, "cq", SQ["cq"])
                project(l, KR, 0, 32)
                spread(l, "cq")
                read(pe, ("tile", l, CKV))
                sums(l, "ckv", SQ["ckv"])
                project(l, QD0, tq)
                spread(l, "ckv")
                project(l, QD1, tq)
                read(pe, ("tile", l, QD0))
                sums(l, "qd0", SQ["qd0"])
                pe.wait_ge(scaled, norm_scaled(l, "cq", 2))
                pe.wait_ge(lora_in, 16 * 4 * (l + 1))
                for h in range(4):
                    dst = claim(("lq", l, h))
                    for c in range(2):
                        for cols, toks in pieces(tq, TOK, tq):
                            mm = pe.matmul(dst[0:96, cols], wuq[:, c, h * 96:(h + 1) * 96], QK[:, c, toks],
                                           start=(c == 0), stop=(c == 1))
                    mm.then_inc(aux_done, 1)
                project(l, KD, 0)
                spread(l, "qd0")
                read(pe, ("tile", l, QD1))
                sums(l, "qd1", SQ["qd1"])
                pe.wait_ge(scaled, norm_scaled(l, "ckv", 1))
                for h in range(4):
                    dst = claim(("lk", l, h))
                    for cols, toks in pieces(0, TOK, 0):
                        mm = pe.matmul(dst[0:64, cols], wukv[:, h * P:h * P + 64], QK[:, 2, toks],
                                       start=True, stop=True)
                    mm.then_inc(aux_done, 1)
                for c in range(2):
                    dst = claim(("lv", l, c))
                    for b in range(4 * c, min(4 * c + 4, NB)):
                        mm = pe.matmul(dst[:, (b - 4 * c) * 256:(b - 4 * c + 1) * 256], QK[:, 2, b * P:(b + 1) * P],
                                       wukv[:, :].rearrange("p (h e) -> p h e", e=P)[:, :, 64:P],
                                       start=True, stop=True)
                    mm.then_inc(aux_done, 1)
                read(pe, ("tile", l, KD))
                sums(l, "kd", SQ["kd"])
                project(l, QA0, tq)
                spread(l, "qd1")
                spread(l, "kd")
                project(l, QA1, tq)
                project(l, KA, 0)

                def maxima(h, blocks):
                    if not blocks:
                        return
                    kind, _, _, _, rows, _ = HEADS[h]
                    for b in blocks:
                        key = ("max", l, h, b)
                        dst = claim(key)
                        if b == query_blocks(l)[0]:
                            pe.wait_ge(casts, 2 * (l * NH + h + 1))
                        q = cast_rows[0:rows, 0, b * P:(b + 1) * P]
                        spans = key_spans(h, b)
                        for s, (c0, k0, n, mask) in enumerate(spans):
                            mm = pe.matmul(dst[:, c0:c0 + n], q, cast_rows[0:rows, 1, k0:k0 + n],
                                           start=True, stop=not mask, skip_group_check=True)
                            for m0, side in mask:
                                mm = pe.matmul(dst[:, m0:m0 + P], id16, upper16 if side == "before" else lower16, start=False, stop=True,
                                               skip_group_check=True)
                        mm.then_inc(aux_done, 1)

                def spread_negmax(h):
                    key = ("negm", l, h)
                    dst = claim(key)
                    pe.wait_ge(diag_ready, l * NH + h + 1)
                    for cols, toks in pieces(tq, TOK, tq):
                        mm = pe.matmul(dst[:, cols], ones16, negm_diag[:, toks], start=True, stop=True)
                    mm.then_inc(aux_done, 1)

                def scores(h, j):
                    kind, q, k, _, rows, _ = HEADS[h]
                    kb = KEYS[j]
                    dst = claim(("s", l, h, j))
                    if j == 0:
                        read(pe, ("negm", l, h))
                    a, b = query_range(l, h, kb)
                    masks = []
                    if kind == "A" and kb >= CB:
                        masks = [(t, m) for t, m in (((kb - 1) * P, upper16), ((kb + 1) * P, lower16))
                                 if a <= t < b and t != kb * P and t >= CTX]
                    for cols, toks in pieces(a, b, tq):
                        inside = [(t, m) for t, m in masks if toks.start <= t < toks.stop]
                        mm = pe.matmul(dst[:, cols], QK[0:rows + 1, k, kb * P:(kb + 1) * P],
                                       QK[0:rows + 1, q, toks], start=True, stop=not inside,
                                       skip_group_check=True)
                        for n, (t, m) in enumerate(inside):
                            mm = pe.matmul(dst[:, t - tq:t - tq + P], id16, m, start=False,
                                           stop=(n == len(inside) - 1), skip_group_check=True)
                    mm.then_inc(aux_done, 1)

                def values(h, j):
                    _, _, _, v, _, _ = HEADS[h]
                    kb = KEYS[j]
                    if j == 0:
                        claim(("o", l, h))
                    dst = ps[PLAN[("o", l, h)][0]]
                    read(pe, ("s", l, h, j))
                    a, b = query_range(l, h, kb)
                    first = v * P + (64 if h % 2 == 0 else 0)
                    lhs = V[:, kb, :, :].rearrange("p v e -> p (v e)")[:, first:first + P]
                    for cols, toks in pieces(a, b, tq):
                        mm = pe.matmul(dst[:, cols], lhs, work[:, j % 2, toks], start=(j == 0),
                                       stop=(j == len(KEYS) - 1), skip_group_check=True)
                    mm.then_inc(pv_done, 1)

                blocks = query_blocks(l)

                def first_maxima(k):
                    pe.wait_ge(krope_spread, 3 * (l + 1))
                    maxima(0, blocks[k:k + 1])

                project(l, UB0, tq)
                project(l, UB1, tq, ready=first_maxima)
                spread_negmax(0)
                pe.wait_ge(v_ones, 4 * (l + 1))
                pe.wait_ge(last_ones, l + 1)
                for h in range(NH):
                    for j in range(len(KEYS)):
                        scores(h, j)
                        ahead = blocks[2 * (j - 2):2 * (j - 1)] if h + 1 < NH and 2 <= j < 5 else []
                        maxima(h + 1, ahead[:1])
                        if j and j < len(KEYS) - 1:
                            values(h, j - 1)
                        maxima(h + 1, ahead[1:])
                    values(h, len(KEYS) - 2)
                    if h + 1 < NH:
                        spread_negmax(h + 1)
                    values(h, len(KEYS) - 1)
                    if h == 1:
                        for c in range(2):
                            key = ("pool", l, c)
                            dst = claim(key)
                            pe.wait_ge(ypool_f, 2 * l + c + 1)
                            u = work[:, 3 if c == 0 else 2, :]
                            if tq:
                                runs = [(slice(0, LAT), 3 * PAD + CTX)]
                            else:
                                runs = [(slice(0, CTX), PAD), (slice(CTX, 512), 3 * PAD + CTX),
                                        (slice(512, TOK), 3 * PAD + 512)]
                            for cols, at in runs:
                                mm = pe.matmul(dst[:, cols], poolw[:, c, :], u[:, at:at + cols.stop - cols.start],
                                               start=True, stop=True)
                            mm.then_inc(aux_done, 1)

                pe.wait_ge(split_done, l * TILES + N_IN + 2)
                dsts = [claim(("tile", l, N_IN + m)) for m in range(2)]
                order = [2, 3, 4, 5, 6, 7, 0, 1]
                for n, k in enumerate(order):
                    pe.wait_ge(head_done, l * NH // 2 + (NH // 2 - 1 + k if k < 2 else NH // 2 - 2))
                    for m in range(2):
                        mm = passes(dsts[m], m, k, pieces(tq, TOK, tq), P, h_hi, h_lo, k, n == 0, n == DC - 1)
                        if n == DC - 1:
                            mm.then_inc(tile_done, 1)
                for m in range(2, N_OUT):
                    project(l, N_IN + m, tq)
                read(pe, ("tile", l, N_IN + N_OUT - 1))
                stream_sums(l, "post1")
                stream_sums(l, "pre2")

                n_s = 1 if last else 2
                los[0] += n_s * DC
                tokens = pieces(tq, TOK, tq)
                f0 = N_IN + N_OUT
                pairs = 0
                for g, ng in enumerate(FG):
                    first = 0
                    if g == 0:
                        first = 1
                        pe.wait_ge(split_done, l * TILES + f0 + 2)
                        dsts = [claim(("tile", l, f0 + m)) for m in range(2)]
                        for k in range(DC):
                            pe.wait_ge(lo_ready, los[0] - n_s * (DC - k - 1))
                            for m in range(2):
                                mm = passes(dsts[m], m, k, tokens, P, h_hi, h_lo, k, k == 0, k == DC - 1)
                                if k == DC - 1:
                                    mm.then_inc(tile_done, 1)
                        for m in range(2, 4):
                            project(l, f0 + m, tq)
                    with pe.Fori(first, ng // 2) as i:
                        for m in range(4):
                            use = PLAN[("tile", l, f0 + m)][1]
                            pe.wait_ge(read_out[m], i + use)
                            pe.wait_ge(split_done, i * 4 + (l * TILES + f0 + m + 1))
                            for k in range(DC):
                                mm = passes(ps[m], m % 2, k, tokens, P, h_hi, h_lo, k, k == 0, k == DC - 1)
                            mm.then_inc(tile_done, 1)
                    f0 += 2 * ng
                    pairs += ng
                    with pe.Fori(0, DC // 4) as i:
                        for m in range(4):
                            use = PLAN[("tile", l, f0 + m)][1]
                            pe.wait_ge(read_out[m], i + use)
                            pe.wait_ge(split_done, i * 4 + (l * TILES + f0 + m + 1))
                            for k in range(ng):
                                if m == 0:
                                    pe.wait_ge(prod_step, l * sum(FG) + pairs - (ng - k - 1))
                                mm = passes(ps[m], m % 2, k, tokens, P, act_hi, act_lo, k, k == 0, k == ng - 1)
                            mm.then_inc(tile_done, 1)
                    f0 += DC
                stream_sums(l, "post2")


def constants(np, bf16):
    k = np.zeros((P, NCONST), np.float32)
    k[:, KID:KID + P] = np.eye(P)
    k[:, KMEAN] = 1 / D
    k[:, KMEAN + 1] = 1 / 256
    k[:, KMEAN + 2] = 1 / 128
    k[0:64, KMEAN + 3] = k[64:P, KMEAN + 4] = 1 / 64
    t = np.arange(LAT)
    row, col = (t // 64).astype(np.float32), (t % 64).astype(np.float32)
    p = np.arange(P)
    rope = np.zeros((P, 4, LAT), np.float32)
    for at, half in ((RHD, 32), (RC, 16)):
        n = half // 2
        freq = (np.float32(10000.0) ** (-np.arange(n, dtype=np.float32) / np.float32(n))).astype(np.float32)
        j = p % half
        pos = np.where((j < n)[:, None], row[None, :], col[None, :])
        ang = (pos * freq[j % n][:, None]).astype(np.float32).astype(np.float64)
        rope[:, at] = np.cos(ang)
        rope[:, at + 1] = np.sin(ang) * np.where((p // half) % 2 == 0, -1.0, 1.0)[:, None]
    for c in range(2):
        for half, size in enumerate(((2, 4), (8, 16))[c]):
            rows = slice(64 * half, 64 * half + 64)
            k[rows, KINV + c] = 1 / size
            for e, (n, first) in enumerate(((CTX, 0), (CTX, CTX - PAD), (LAT, 0), (LAT, LAT - PAD))):
                pos = np.arange(first, first + PAD)
                lo, hi = np.clip(pos - size // 2, 0, n), np.clip(pos - size // 2 + size, 0, n)
                at = KEDGE + (c * 4 + e) * PAD
                k[rows, at:at + PAD] = size / (hi - lo)
    b = np.zeros((P, 4, P), np.float32)
    i, f = np.arange(P)[:, None], np.arange(P)[None, :]
    b[:, 0] = np.eye(P)
    b[:, 1] = np.where(f >= i, 0, -1e30)
    b[:, 2] = np.where(f <= i, 0, -1e30)
    b[:, 3] = 1
    return k, b.astype(bf16), rope


def layout(np, bf16, v):
    L = LAYERS

    def tiles(w):
        l, kk, n = w.shape
        w = w.reshape(l, kk // P, P, n // P, P).transpose(0, 3, 2, 1, 4)
        if kk // P < DC:
            w = np.concatenate([w, np.zeros(w.shape[:3] + (DC - kk // P, P), w.dtype)], axis=3)
        return w

    w = v["w_in"]
    cols = {VA: 384, VD: 1568, CQ0: 768, CQ1: 896, CKV: 1024, KR: 1152, QD0: 1184, QD1: 1312, KD: 1440,
            QA0: 0, QA1: 128, KA: 256, UB0: 512, UB1: 640}
    parts = [tiles(w[:, :, cols[i]:cols[i] + P]) for i in range(N_IN)]
    parts.append(tiles(v["w_out"]))
    gate, up = tiles(v["w_gu"][:, :, :FF]), tiles(v["w_gu"][:, :, FF:])
    j = 0
    for ng in FG:
        pair = np.stack([gate[:, j:j + ng], up[:, j:j + ng]], axis=2)
        parts.append(pair.reshape(L, 2 * ng, P, DC, P))
        parts.append(tiles(v["w_down"][:, j * P:(j + ng) * P]))
        j += ng
    stream = np.concatenate(parts, axis=1).reshape(L * TILES, P, DC, P)

    def columns(a):
        return a.reshape(L, -1, P).transpose(2, 0, 1)

    def twice(a):
        return columns(np.concatenate([a, a], axis=1))

    params = np.concatenate(
        [columns(v[g]) for g in ("g_pre1", "g_post1", "g_pre2", "g_post2")]
        + [columns(v["b_ada"]), columns(v["pool_scale"]), columns(v["c_gq"]), columns(v["c_gkv"]),
           twice(v["d_gq"]), twice(v["d_gk"]), np.broadcast_to(v["a_sink"][None], (P, L, 4))], axis=2)
    x_t = np.concatenate([v["ctx"][0], v["x"][0]], axis=0).T.reshape(DC, P, TOK).transpose(1, 0, 2)
    ada_first = tiles(v["w_ada"][:1, :, D:2 * D])[0].transpose(1, 0, 2, 3)
    ada = v["w_ada"].transpose(0, 2, 1).reshape(L * ADA, P, D)
    ada = np.concatenate([ada[:DC], ada[2 * DC:]], axis=0)
    cond = np.concatenate([v["c"], v["c_ctx"][None]], axis=0)
    k, kb, rope = constants(np, bf16)
    blocks = np.zeros((L, P, 2, P), np.float32)
    for g in range(4):
        q = 64 * (g % 2)
        blocks[:, q:q + 64, g // 2, q:q + 64] = v["pool_w"][:, g]
    out = {
        "x_t": x_t, "cond": cond, "cond_t": cond.reshape(2, DC, P).transpose(2, 1, 0),
        "ada_first": ada_first, "ada_t": ada, "stream": stream,
        "params": params, "wuq_t": v["c_wuq"].reshape(L, 2, P, 384).transpose(0, 2, 1, 3),
        "wukv_t": v["c_wukv"], "pool_w": blocks, "consts": k, "consts_b": kb, "rope_t": rope,
    }
    return {n: np.ascontiguousarray(a) for n, a in out.items()}


def kernel(**inputs):
    import ml_dtypes
    import numpy as np
    import concourse.bacc as bacc
    from concourse.bass_utils import run_bass_kernel_spmd

    v = {n: np.asarray(a) for n, a in inputs.items()}
    arrays = layout(np, ml_dtypes.bfloat16, v)
    nc = bacc.Bacc("TRN2", target_bir_lowering=False, num_devices=1, dynamic_dma_scratch_size=1024)
    args = [nc.dram_tensor(n, a.shape, mybir.dt.from_np(a.dtype), kind="ExternalInput").ap()
            for n, a in arrays.items()]
    args.append(nc.dram_tensor("out_t", (P, DC, LAT), F32, kind="ExternalOutput").ap())
    build(nc, *args)
    r = run_bass_kernel_spmd(nc, [arrays], core_ids=[0])
    out = np.asarray(r.results[0]["out_t"])
    return np.ascontiguousarray(out.transpose(2, 1, 0).reshape(1, LAT, D))
```
